# Optimizing a Trainium2 kernel written in Bass

```python
import jax, jax.numpy as jnp
from jax import lax
import numpy as np

D_MODEL = 1024
BATCH = 1
SEQ = 256
DEPTH = 2
DEC_BATCH = 1
DEC_SEQ = 256
PAST_LEN = 128

PLE_DIM = 256
N_MIXERS = 2
N_MLA_LAYERS = (DEPTH + 1) // 2
N_GDN_LAYERS = DEPTH // 2
MLA_HEADS = 8
MLA_NOPE_DIM = 128
MLA_ROPE_DIM = 64
MLA_V_DIM = 128
MLA_Q_LORA = 256
MLA_KV_LORA = 128
MLA_IN_DIM = MLA_Q_LORA + MLA_KV_LORA + MLA_ROPE_DIM
ROPE_THETA = 10000.0
Q_BLOCK = 128
GDN_HEADS = 8
GDN_DK = 128
GDN_DV = 128
GDN_CONV = 5
GDN_CHUNK = 64
GDN_QKV_DIM = 2 * GDN_HEADS * GDN_DK + GDN_HEADS * GDN_DV
GDN_IN_DIM = GDN_QKV_DIM + GDN_HEADS * GDN_DV + 4 * GDN_HEADS
N_EXPERTS = 16
D_EXPERT = 1024
EC_CAPACITY_FACTOR = 2
NORM_EPS = 1e-6

kernel_name = 'hybrid_mla_gdn_ec_encoder'

def rmsnorm(x, g):
    x32 = x.astype(jnp.float32)
    y = x32 * lax.rsqrt(jnp.mean(x32 * x32, axis=-1, keepdims=True) + NORM_EPS)
    return (y * g.astype(jnp.float32)).astype(x.dtype)

def l2norm(x):
    x32 = x.astype(jnp.float32)
    return x32 * lax.rsqrt(jnp.sum(x32 * x32, axis=-1, keepdims=True) + NORM_EPS)

def rope_tables(seq):
    pos = jnp.arange(seq, dtype=jnp.float32)
    inv = ROPE_THETA ** (-jnp.arange(0, MLA_ROPE_DIM, 2, dtype=jnp.float32) / MLA_ROPE_DIM)
    ang = pos[:, None] * inv[None, :]
    return jnp.cos(ang), jnp.sin(ang)

def apply_rope(x, cos, sin):
    half = x.shape[-1] // 2
    x1, x2 = x[..., :half], x[..., half:]
    return jnp.concatenate([x1 * cos - x2 * sin, x2 * cos + x1 * sin], axis=-1)

def mla_mixer(h, w_in, q_norm_g, w_qb, kv_norm_g, w_kvb, w_out):
    B, S, _ = h.shape
    H = MLA_HEADS
    lat = h @ w_in
    q_lat = lat[..., :MLA_Q_LORA]
    kv_lat = lat[..., MLA_Q_LORA:MLA_Q_LORA + MLA_KV_LORA]
    k_rope = lat[..., MLA_Q_LORA + MLA_KV_LORA:]
    q = (rmsnorm(q_lat, q_norm_g) @ w_qb).reshape(B, S, H, MLA_NOPE_DIM + MLA_ROPE_DIM)
    q_nope, q_rope = q[..., :MLA_NOPE_DIM], q[..., MLA_NOPE_DIM:]
    kv = (rmsnorm(kv_lat, kv_norm_g) @ w_kvb).reshape(B, S, H, MLA_NOPE_DIM + MLA_V_DIM)
    k_nope, v = kv[..., :MLA_NOPE_DIM], kv[..., MLA_NOPE_DIM:]
    cos, sin = rope_tables(S)
    cos, sin = cos.astype(h.dtype), sin.astype(h.dtype)
    q_rope = apply_rope(q_rope, cos[:, None, :], sin[:, None, :])
    k_rope = apply_rope(k_rope, cos, sin)
    scale = (MLA_NOPE_DIM + MLA_ROPE_DIM) ** -0.5
    nb = S // Q_BLOCK
    qn_b = q_nope.reshape(B, nb, Q_BLOCK, H, MLA_NOPE_DIM).transpose(1, 0, 2, 3, 4)
    qr_b = q_rope.reshape(B, nb, Q_BLOCK, H, MLA_ROPE_DIM).transpose(1, 0, 2, 3, 4)

    def query_block(args):
        qn, qr = args
        s = jnp.einsum('bqhd,bkhd->bhqk', qn, k_nope) + jnp.einsum('bqhr,bkr->bhqk', qr, k_rope)
        pr = jax.nn.softmax(s.astype(jnp.float32) * scale, axis=-1).astype(v.dtype)
        return jnp.einsum('bhqk,bkhd->bqhd', pr, v)

    o = lax.map(query_block, (qn_b, qr_b))
    o = o.transpose(1, 0, 2, 3, 4).reshape(B, S, H * MLA_V_DIM)
    return o @ w_out

def centred_short_conv(x, w):
    S = x.shape[1]
    pad = GDN_CONV // 2
    xp = jnp.pad(x, ((0, 0), (pad, pad), (0, 0)))
    out = xp[:, 0:S, :] * w[0]
    for j in range(1, GDN_CONV):
        out = out + xp[:, j:j + S, :] * w[j]
    return out

def chunk_gated_delta(q, k, v, beta, g):
    B, S, H, DK = q.shape
    DV = v.shape[-1]
    C = GDN_CHUNK
    N = S // C

    def to_chunks(t):
        return t.reshape(B, N, C, H, t.shape[-1]).transpose(0, 3, 1, 2, 4)

    q, k, v = to_chunks(q), to_chunks(k), to_chunks(v)
    beta = beta.reshape(B, N, C, H).transpose(0, 3, 1, 2)
    g = g.reshape(B, N, C, H).transpose(0, 3, 1, 2)
    gc = jnp.cumsum(g, axis=-1)
    idx = jnp.arange(C)
    incl = idx[:, None] >= idx[None, :]
    strict = idx[:, None] > idx[None, :]
    diff = gc[..., :, None] - gc[..., None, :]
    decay = jnp.where(incl, jnp.exp(jnp.where(incl, diff, 0.0)), 0.0)
    kb = k * beta[..., None]
    vb = v * beta[..., None]
    L = jnp.where(strict, jnp.einsum('bhncd,bhnsd->bhncs', kb, k) * decay, 0.0)
    eye = jnp.eye(C, dtype=jnp.float32)
    T = lax.linalg.triangular_solve(eye + L, jnp.broadcast_to(eye, L.shape), left_side=True, lower=True)
    u = T @ vb
    w = T @ (kb * jnp.exp(gc)[..., None])
    a_intra = jnp.einsum('bhncd,bhnsd->bhncs', q, k) * decay
    q_g = q * jnp.exp(gc)[..., None]
    k_g = k * jnp.exp(gc[..., -1:] - gc)[..., None]
    g_last = jnp.exp(gc[..., -1])
    xs = (jnp.moveaxis(u, 2, 0), jnp.moveaxis(w, 2, 0), jnp.moveaxis(a_intra, 2, 0),
          jnp.moveaxis(q_g, 2, 0), jnp.moveaxis(k_g, 2, 0), jnp.moveaxis(g_last, 2, 0))

    def step(state, inp):
        u_n, w_n, a_n, qg_n, kg_n, gl_n = inp
        v_new = u_n - w_n @ state
        o_n = qg_n @ state + a_n @ v_new
        state = state * gl_n[..., None, None] + jnp.swapaxes(kg_n, -1, -2) @ v_new
        return state, o_n

    state0 = jnp.zeros((B, H, DK, DV), jnp.float32)
    _, o = lax.scan(step, state0, xs)
    return o.transpose(1, 0, 3, 2, 4).reshape(B, S, H, DV)

def gdn_mixer(h, w_in, conv_w, A_log, dt_bias, norm_g, w_out):
    B, S, _ = h.shape
    H = GDN_HEADS
    proj = h @ w_in
    qkv = proj[..., :GDN_QKV_DIM]
    z = proj[..., GDN_QKV_DIM:GDN_QKV_DIM + H * GDN_DV]
    b = proj[..., GDN_QKV_DIM + H * GDN_DV:GDN_QKV_DIM + H * GDN_DV + 2 * H]
    a = proj[..., GDN_QKV_DIM + H * GDN_DV + 2 * H:]
    qkv = jax.nn.silu(centred_short_conv(qkv, conv_w))
    q = l2norm(qkv[..., :H * GDN_DK].reshape(B, S, H, GDN_DK)) * (GDN_DK ** -0.5)
    k = l2norm(qkv[..., H * GDN_DK:2 * H * GDN_DK].reshape(B, S, H, GDN_DK))
    v = qkv[..., 2 * H * GDN_DK:].reshape(B, S, H, GDN_DV).astype(jnp.float32)
    beta = jax.nn.sigmoid(b.astype(jnp.float32)).reshape(B, S, 2, H)
    g = -jnp.exp(A_log.astype(jnp.float32)) * jax.nn.softplus(
        a.astype(jnp.float32).reshape(B, S, 2, H) + dt_bias.astype(jnp.float32))
    o_fwd = chunk_gated_delta(q, k, v, beta[:, :, 0], g[:, :, 0])
    o_bwd = jnp.flip(chunk_gated_delta(jnp.flip(q, 1), jnp.flip(k, 1), jnp.flip(v, 1),
                                       jnp.flip(beta[:, :, 1], 1), jnp.flip(g[:, :, 1], 1)), 1)
    o = (o_fwd + o_bwd).astype(h.dtype)
    o = rmsnorm(o, norm_g) * jax.nn.silu(z.reshape(B, S, H, GDN_DV))
    return o.reshape(B, S, H * GDN_DV) @ w_out

def expert_choice_moe(h, w_router, w_gate, w_up, w_down):
    B, S, D = h.shape
    T = B * S
    cap = EC_CAPACITY_FACTOR * T // N_EXPERTS
    xt = h.reshape(T, D)
    aff = jax.nn.softmax((xt @ w_router).astype(jnp.float32), axis=-1)
    gate, idx = lax.top_k(aff.T, cap)
    xe = jnp.take(xt, idx, axis=0)
    hid = jax.nn.silu(jnp.einsum('ecd,edf->ecf', xe, w_gate)) * jnp.einsum('ecd,edf->ecf', xe, w_up)
    ye = jnp.einsum('ecf,efd->ecd', hid, w_down) * gate[..., None].astype(h.dtype)
    out = jnp.zeros_like(xt).at[idx.reshape(-1)].add(ye.reshape(-1, D))
    return out.reshape(B, S, D)

def encoder_trunk(x, p, W):
    h = x
    for i in range(DEPTH):
        hn = rmsnorm(h, W['norm_mix_g'][i])
        j = i // N_MIXERS
        if i % N_MIXERS == 0:
            h = h + mla_mixer(hn, W['mla_w_in'][j], W['mla_q_norm_g'][j], W['mla_w_qb'][j],
                              W['mla_kv_norm_g'][j], W['mla_w_kvb'][j], W['mla_w_out'][j])
        else:
            h = h + gdn_mixer(hn, W['gdn_w_in'][j], W['gdn_conv_w'][j], W['gdn_A_log'][j],
                              W['gdn_dt_bias'][j], W['gdn_norm_g'][j], W['gdn_w_out'][j])
        h = h + expert_choice_moe(rmsnorm(h, W['norm_ffn_g'][i]), W['moe_w_router'][i],
                                  W['moe_w_gate'][i], W['moe_w_up'][i], W['moe_w_down'][i])
        gate = jax.nn.sigmoid(rmsnorm(h, W['norm_ple_g'][i]) @ W['ple_w_gate'][i])
        h = h + (p[i] @ W['ple_w_proj'][i]) * gate
    return rmsnorm(h, W['final_norm_g'])

def setup_inputs(seed: int = 0) -> dict:
    key = jax.random.key(seed)
    ks = jax.random.split(key, 26)
    f32 = jnp.float32

    def nrm(k, shape, fan_in):
        return jax.random.normal(k, shape, f32) * (fan_in ** -0.5)

    def gain(k, shape):
        return 1.0 + 0.05 * jax.random.normal(k, shape, f32)

    dt = jnp.exp(jax.random.uniform(ks[17], (N_GDN_LAYERS, 2, GDN_HEADS), f32,
                                    float(np.log(1e-3)), float(np.log(1e-1))))
    return {
        'x_prompt': jax.random.normal(ks[0], (BATCH, SEQ, D_MODEL), f32),
        'x_sample': jax.random.normal(ks[1], (DEC_BATCH, DEC_SEQ, D_MODEL), f32),
        'p_prompt': jax.random.normal(ks[2], (DEPTH, BATCH, SEQ, PLE_DIM), f32),
        'p_sample': jax.random.normal(ks[3], (DEPTH, DEC_BATCH, DEC_SEQ, PLE_DIM), f32),
        'norm_mix_g': gain(ks[4], (DEPTH, D_MODEL)),
        'norm_ffn_g': gain(ks[5], (DEPTH, D_MODEL)),
        'norm_ple_g': gain(ks[6], (DEPTH, D_MODEL)),
        'final_norm_g': gain(ks[7], (D_MODEL,)),
        'mla_w_in': nrm(ks[8], (N_MLA_LAYERS, D_MODEL, MLA_IN_DIM), D_MODEL),
        'mla_q_norm_g': gain(ks[9], (N_MLA_LAYERS, MLA_Q_LORA)),
        'mla_w_qb': nrm(ks[10], (N_MLA_LAYERS, MLA_Q_LORA, MLA_HEADS * (MLA_NOPE_DIM + MLA_ROPE_DIM)), MLA_Q_LORA),
        'mla_kv_norm_g': gain(ks[11], (N_MLA_LAYERS, MLA_KV_LORA)),
        'mla_w_kvb': nrm(ks[12], (N_MLA_LAYERS, MLA_KV_LORA, MLA_HEADS * (MLA_NOPE_DIM + MLA_V_DIM)), MLA_KV_LORA),
        'mla_w_out': nrm(ks[13], (N_MLA_LAYERS, MLA_HEADS * MLA_V_DIM, D_MODEL), MLA_HEADS * MLA_V_DIM),
        'gdn_w_in': nrm(ks[14], (N_GDN_LAYERS, D_MODEL, GDN_IN_DIM), D_MODEL),
        'gdn_conv_w': nrm(ks[15], (N_GDN_LAYERS, GDN_CONV, GDN_QKV_DIM), GDN_CONV),
        'gdn_A_log': jnp.log(jax.random.uniform(ks[16], (N_GDN_LAYERS, 2, GDN_HEADS), f32, 1.0, 16.0)),
        'gdn_dt_bias': dt + jnp.log(-jnp.expm1(-dt)),
        'gdn_norm_g': gain(ks[18], (N_GDN_LAYERS, GDN_DV)),
        'gdn_w_out': nrm(ks[19], (N_GDN_LAYERS, GDN_HEADS * GDN_DV, D_MODEL), GDN_HEADS * GDN_DV),
        'moe_w_router': nrm(ks[20], (DEPTH, D_MODEL, N_EXPERTS), D_MODEL),
        'moe_w_gate': nrm(ks[21], (DEPTH, N_EXPERTS, D_MODEL, D_EXPERT), D_MODEL),
        'moe_w_up': nrm(ks[22], (DEPTH, N_EXPERTS, D_MODEL, D_EXPERT), D_MODEL),
        'moe_w_down': nrm(ks[23], (DEPTH, N_EXPERTS, D_EXPERT, D_MODEL), D_EXPERT),
        'ple_w_proj': nrm(ks[24], (DEPTH, PLE_DIM, D_MODEL), PLE_DIM),
        'ple_w_gate': nrm(ks[25], (DEPTH, D_MODEL, D_MODEL), D_MODEL),
    }

def reference(x_prompt, x_sample, p_prompt, p_sample, norm_mix_g, norm_ffn_g, norm_ple_g, final_norm_g,
              mla_w_in, mla_q_norm_g, mla_w_qb, mla_kv_norm_g, mla_w_kvb, mla_w_out,
              gdn_w_in, gdn_conv_w, gdn_A_log, gdn_dt_bias, gdn_norm_g, gdn_w_out,
              moe_w_router, moe_w_gate, moe_w_up, moe_w_down, ple_w_proj, ple_w_gate):
    W = {
        'norm_mix_g': norm_mix_g, 'norm_ffn_g': norm_ffn_g, 'norm_ple_g': norm_ple_g,
        'final_norm_g': final_norm_g,
        'mla_w_in': mla_w_in, 'mla_q_norm_g': mla_q_norm_g, 'mla_w_qb': mla_w_qb,
        'mla_kv_norm_g': mla_kv_norm_g, 'mla_w_kvb': mla_w_kvb, 'mla_w_out': mla_w_out,
        'gdn_w_in': gdn_w_in, 'gdn_conv_w': gdn_conv_w, 'gdn_A_log': gdn_A_log,
        'gdn_dt_bias': gdn_dt_bias, 'gdn_norm_g': gdn_norm_g, 'gdn_w_out': gdn_w_out,
        'moe_w_router': moe_w_router, 'moe_w_gate': moe_w_gate, 'moe_w_up': moe_w_up,
        'moe_w_down': moe_w_down, 'ple_w_proj': ple_w_proj, 'ple_w_gate': ple_w_gate,
    }
    y_prompt = encoder_trunk(x_prompt, p_prompt, W)
    y_sample = encoder_trunk(x_sample, p_sample, W)
    return (y_prompt, y_sample)


_drawn_inputs = setup_inputs


def setup_inputs(seed=0):
    import zlib

    import numpy as np

    out = dict(_drawn_inputs(seed))
    spreads = {}
    factors = {'norm_ple_g': 15.699,
     'mla_q_norm_g': 4.385,
     'mla_kv_norm_g': 3.008,
     'norm_ffn_g': 3.739,
     'gdn_norm_g': 5.329}
    for name, (base, spread) in spreads.items():
        noise = np.random.default_rng([zlib.crc32(name.encode()), seed]).standard_normal(out[name].shape)
        drawn = base * np.exp(spread * noise) if base else spread * noise
        out[name] = __import__('jax').numpy.asarray(drawn.astype(out[name].dtype))
    for name, factor in factors.items():
        out[name] = (out[name] * factor).astype(out[name].dtype)
    return out
```

```python
from contextlib import ExitStack

import numpy as np

import concourse.bass as bass
from concourse import mybir

P = 128
F32 = mybir.dt.float32
U32 = mybir.dt.uint32
ALU = mybir.AluOpType
ACT = mybir.ActivationFunctionType
AX_X = mybir.AxisListType.X

D = 1024
KD = D // P
NS = 2
SEQ = 256
T = NS * SEQ
NJ = T // P
NT = SEQ // P
EPS = 1e-6
HEADS = 8
NOPE, ROPE, DV = 128, 64, 128
QL, KVL = 256, 128
LAT = QL + KVL + ROPE
SCALE = (NOPE + ROPE) ** -0.5
PLE = 256
NE = 16
FE = 1024
CAP = 2 * SEQ // NE
NSLOT = 8
SLOTW = 4096
HALF = 512
GRP = 4
NQ = NE // GRP
LAYERS = range(2)
NBANK = 8

ROW_MIX, ROW_FFN, ROW_PLE, ROW_QN, ROW_KVN = 0, 16, 32, 48, 50
ROW_GDN = 51
NROWS = 52

GH = 8
CONV = 5
GQKV = 3 * D
LEVELS = 7
TRI_LE, TRI_GE, TRI_GT, TRI_LT = range(4)
F_G, F_BETA, F_NBETA, F_EG, F_BEG, F_KG, F_X, F_Y = range(8)


class Stage:

    def __init__(self, sem, name, n, readers, before=None):
        self.name, self.n, self.readers = name, n, readers
        self.filled = before.filled if before else sem(name + "_in_psum")
        self.read = before.read if before else {r: sem(f"{name}_read_{r}") for r in dict.fromkeys(readers)}
        self.past = before.past + before.n if before else 0
        self.past_read = {r: before.freed(max(i for i in range(before.n) if before.reader(i) == r))[1] if before else 0
                          for r in self.read}
        self.at = {}

    def full(self, count):
        return self.filled, self.past + count

    def reader(self, i):
        return self.readers[i % len(self.readers)]

    def freed(self, i):
        r = self.reader(i)
        per = self.readers.count(r)
        before = [x for x in range(i % len(self.readers)) if self.readers[x] == r]
        return self.read[r], self.past_read[r] + (i // len(self.readers)) * per + len(before) + 1

    def wait_read(self, eng, upto):
        need = {}
        for i in range(max(0, upto + 1 - len(self.readers)), upto + 1):
            s, c = self.freed(i)
            need[self.reader(i)] = (s, c)
        for s, c in need.values():
            eng.wait_ge(s, c)


class Ring:

    def __init__(self):
        self.order = []

    def add(self, stage, i):
        stage.at[i] = len(self.order)
        self.order.append((stage, i))

    def bank(self, stage, i):
        return stage.at[i] % NBANK

    def claim(self, pe, stage, i):
        at = stage.at[i] - NBANK
        if at >= 0:
            before, n = self.order[at]
            s, c = before.freed(n)
            pe.wait_ge(s, c)


def trunk_kernel(nc, x_prompt, x_sample, p_prompt, p_sample, norm_mix_g, norm_ffn_g, norm_ple_g,
                 final_norm_g, mla_w_in, mla_q_norm_g, mla_w_qb, mla_kv_norm_g, mla_w_kvb, mla_w_out,
                 gdn_w_in, gdn_conv_w, gdn_A_log, gdn_dt_bias, gdn_norm_g, gdn_w_out,
                 moe_w_router, moe_w_gate, moe_w_up, moe_w_down, ple_w_proj, ple_w_gate,
                 rope_cos, rope_sin, y_prompt, y_sample):
    with ExitStack() as ctx:
        def sb(name, shape, dt=F32):
            return ctx.enter_context(nc.sbuf_tensor(name, shape, dt))

        def sem(name):
            return ctx.enter_context(nc.semaphore(name))

        ring = sb("ring", [P, NSLOT, SLOTW])
        h = sb("h", [P, NJ, D])
        xn = sb("xn", [P, NJ, D])
        xt = sb("xt", [P, KD, T])
        misc = sb("misc", [P, 6144])
        work = sb("work", [P, D])
        ident = sb("ident", [P, P])
        ones = sb("ones", [P, P])
        diag32 = sb("diag32", [32, 32])
        token = sb("token", [P, NT])
        gains = sb("gains", [P, 64])
        ss = sb("ss", [P, 32])
        rs = sb("rs", [P, 32])
        eps = sb("eps", [P, 1])
        q_eps = sb("q_eps", [P, 1])
        cs = sb("cs", [P, 2, NT, ROPE // 2])
        wr = sb("wr", [P, 2, KD, NE])
        tri = sb("tri", [P, 4, P])
        blocks = sb("blocks", [P, 2 * LEVELS, P], mybir.dt.uint8)
        conv_w = sb("conv_w", [P, CONV * 24])
        wba = sb("wba", [P, KD, 32])
        ba = sb("ba", [P, NJ, 32])
        fac = sb("fac", [P, 8, NJ, 16])
        alog = sb("alog", [P, 2, 16])
        psum = ctx.enter_context(nc.psum_tensor("banks", [P, NBANK, HALF], F32))

        def slot(n, k, w):
            return ring[:, n, 0:k * w].rearrange("p (k w) -> p k w", k=k)

        lat = misc[:, 0:NJ * LAT].rearrange("p (j w) -> p j w", j=NJ)
        kvt = misc[:, 1792:1792 + T]
        krt = misc[:, 2304:2304 + T]
        prob = misc[:, 2816:3840].rearrange("p (b w) -> p b w", b=2)
        pt = misc[:, 3840:4864].rearrange("p (b w) -> p b w", b=2)
        krd = misc[:, 4864:5376].rearrange("p (j w) -> p j w", j=NJ)
        rt1 = misc[:, 5376:5504].rearrange("p (j w) -> p j w", j=NJ)
        rt2 = misc[:, 5504:5632].rearrange("p (j w) -> p j w", j=NJ)
        w_lat, w_qb, w_kvb = slot(0, KD, LAT), slot(1, 2, 1536), ring[:, 2, 0:2048]
        w_mo = [slot(3, HEADS, HALF), slot(4, HEADS, HALF)]
        qlt = ring[:, 1, 3072:4096].rearrange("p (k t) -> p k t", k=2)
        qrt = ring[:, 2, 2048:4096].rearrange("p (k t) -> p k t", k=4)
        qt, kt, vv = slot(5, HEADS, T), slot(6, HEADS, T), slot(7, NJ, D)
        qrn = xt[:, 0:4, :].rearrange("p k t -> p (k t)").rearrange("p (j w) -> p j w", j=NJ)
        qrr = xt[:, 4:8, :].rearrange("p k t -> p (k t)").rearrange("p (j w) -> p j w", j=NJ)
        ot = xn[:, :, :].rearrange("p j d -> p (j d)").rearrange("p (h t) -> p h t", h=HEADS)

        rows = misc[0:64, 5632:5760]

        oh = xt[:, 0:4, :]
        sc = xt[:, 4:8, :].rearrange("p q (j t) -> p q j t", j=NJ)
        xe = misc[:, 0:2048].rearrange("p (k e s c) -> p k e s c", k=KD, e=GRP, s=NS)
        ybuf = misc[:, 2048:4096].rearrange("p (s d) -> p s d", s=NS)
        hid = misc[:, 4096:5120].rearrange("p (b f) -> p b f", b=2)
        sg = misc[:, 5120:6144].rearrange("p (b f) -> p b f", b=2)
        scs = work[:, 512:1024].rearrange("p (j t) -> p j t", j=NJ)
        aff = work[:, 0:64].rearrange("p (n s e) -> p n s e", n=NT, s=NS)
        afft = work[0:32, 64:320]
        topv = sb("topv", [32, CAP])
        topi = sb("topi", [32, CAP], U32)
        topf = sb("topf", [32, CAP])
        gcol = sb("gcol", [64, NE])
        gstep = sb("gstep", [64, GRP])
        spread = misc[0:32, 4096:5120].rearrange("p (a c) -> p a c", c=CAP)

        pin = misc[:, 0:1024].rearrange("p (j w) -> p j w", j=NJ)
        ptt = misc[:, 1024:2048].rearrange("p (k t) -> p k t", k=2)
        gate = misc[:, 2048:3072].rearrange("p (b w) -> p b w", b=2)
        prod = misc[:, 3072:4096].rearrange("p (b w) -> p b w", b=2)

        qkv = ring[:, 0:3, :].rearrange("p a w -> p (a w)").rearrange("p (c t) -> p c t", c=24)
        knat, vnat, znat = (slot(a, NJ, D).rearrange("p j (h w) -> p j h w", h=GH) for a in (3, 4, 5))
        pad = misc[:, 0:1040].rearrange("p (b s w) -> p b s w", b=2, s=NS)
        cacc = misc[:, 1040:2064].rearrange("p (b s w) -> p b s w", b=2, s=NS)
        sqb = misc[:, 2064:3088].rearrange("p (b w) -> p b w", b=2)
        rtb = misc[:, 3088:4112].rearrange("p (b w) -> p b w", b=2)
        conv_rows = misc[0:CONV * 24, 4112:4240]

        b_n_sq = misc[:, 0:1024].rearrange("p (h w) -> p h w", h=GH)

        def lanes(buf):
            return [buf(s).rearrange("p (h w) -> p h w", h=4) for s in range(NS)]

        b_gm, b_et, b_at, b_lt, b_n, b_u, b_t, b_z = (
            lanes(lambda s: ring[:, 6 + s, a * HALF:(a + 1) * HALF]) for a in range(8))
        b_r, b_kg, b_vn, b_s, b_tmp = (
            lanes(lambda s: misc[:, (5 * s + a) * HALF:(5 * s + a + 1) * HALF]) for a in range(5))
        o_acc = xn[:, :, :].rearrange("p j (h w) -> p j h w", h=GH)
        gw_out = [slot(2, KD, HALF), xt[:, :, :]]
        got = misc[:, 0:4096].rearrange("p (h t) -> p h t", h=HEADS)
        fg = misc[:, 5120:6144]

        banks = Ring()
        AV = ["act", "dve"]

        def stage(name, n, readers, add=True, before=None):
            st = Stage(sem, name, n, readers, before)
            if add:
                for i in range(n):
                    banks.add(st, i)
            return st

        s_vec = stage("gains", 2, ["dve"])
        s_xt0 = stage("xt", KD, AV)
        s_lat = stage("lat", NJ, AV)
        s_lt = stage("turned", 4, ["dve"])
        s_qn = stage("heads", HEADS, AV)
        s_qr = stage("q_rope", NJ, ["act"])
        s_kn = stage("k_nope", HEADS, AV, before=s_qn)
        s_v = stage("values", 2 * NJ, AV, before=s_kn)
        s_qrt = stage("q_rope_t", 4, ["dve"], before=s_lt)
        s_sc = stage("scores", 16, ["act"], add=False)
        s_pt = stage("prob_t", 16, ["dve"], add=False)
        s_ot = stage("attn_out", 16, ["act"], add=False)
        for i in range(16 + 2):
            if i < 16:
                banks.add(s_sc, i)
            if 1 <= i < 17:
                banks.add(s_pt, i - 1)
            if i >= 2:
                banks.add(s_ot, i - 2)
        s_mo = stage("mixer_proj", 2 * NJ, ["dve"])

        rounds = [(d, f, m) for d in range(2) for f in range(2) for m in range(2)]

        def gidx(r, s):
            return 2 * r + s

        def core_order():
            for r, (d, f, m) in enumerate(rounds):
                for name in ("decay", "kk", "qk", "lt", "n0"):
                    for s in range(NS):
                        yield name, gidx(r, s)
                for v in range(1, LEVELS):
                    for s in range(NS):
                        yield "z", 12 * r + 2 * (v - 1) + s
                    for s in range(NS):
                        if v < LEVELS - 1:
                            yield "dt", 10 * r + 2 * (v - 1) + s
                        yield "du", 12 * r + 2 * (v - 1) + s
                names = ("vn", "av", "st") if m == 0 else ("ks", "vn", "qs", "av")
                for name in names:
                    for s in range(NS):
                        yield name, (2 * (r // 2) + s if name in ("ks", "qs", "st") else gidx(r, s))

        class Layer:
            pass

        PER_LAYER = {"hid_free": NE, "silu_done": NE, "gu_in_psum": 4 * NE, "gather_in_psum": 4 * NQ,
                     "gather_read_act": 8 * NQ, "gather_read_dve": 8 * NQ, "y_in_psum": 2 * NE, "y_free_act": 2 * NE,
                     "y_free_dve": 2 * NE, "scat_in_psum": 8 * NQ, "scat_free": 8 * NQ, "sc_staged": NQ, "gate_staged": NQ}
        moe_sem = {n: sem(n) for n in PER_LAYER}

        lay = []
        for l in range(2):
            L = Layer()
            lay.append(L)
            L.rot = 3 * l
            prev = lay[0] if l else None
            if l == 1:
                s_xt1 = stage("xt", KD, AV, before=prev.s_pxt)
                s_qkv = stage("gdn_qkv", 24, ["act"])
                s_z = stage("gdn_z", 8, ["act"], before=s_qkv)
                s_ba = stage("gdn_ba", 1, ["dve"])
                s_cum = stage("decay_sums", 1, ["act"])
                s_nrm = stage("qk_norm", 16, ["act"])
                s_kt = stage("k_natural", GH, ["act"])
                s_vt = stage("v_natural", GH, ["dve"], before=s_qrt)
                core = {}
                for name, per, reader in (("decay", 1, "act"), ("kk", 1, "dve"), ("qk", 1, "dve"), ("lt", 1, "dve"),
                                          ("n0", 1, "dve"), ("z", 6, "act"), ("dt", 5, "dve"), ("du", 6, "dve"),
                                          ("ks", 1, "dve"), ("vn", 1, "act"), ("av", 1, "dve"), ("qs", 1, "dve"),
                                          ("st", 1, "act")):
                    few = name in ("ks", "qs", "st")
                    core[name] = stage("core_" + name, 16 * per // (2 if few else 1), [reader], add=False)
                for name, i in core_order():
                    banks.add(core[name], i)
                s_av = core["av"]
                s_gt = stage("gdn_out_t", KD, AV, before=s_v)
                s_go = stage("gdn_proj", 2 * NJ, ["dve"], before=s_mo)
            L.s_xt = stage("ffn_xt", KD, AV, before=s_xt1 if l else s_xt0)
            L.s_lg = stage("router", NJ, ["dve"], before=prev and prev.s_ib)
            L.s_at = stage("aff_t", 1, ["dve"], before=L.s_lg)
            L.s_gt = stage("top_t", 1, ["dve"], before=L.s_at)
            L.s_ib = stage("idx_rows", 2, ["dve"], before=L.s_gt)
            L.s_st = stage("scatter_t", 4, AV, before=prev and prev.s_st)
            L.done = {n: l * c for n, c in PER_LAYER.items()}
            L.s_pxt = stage("ple_xt", KD, AV, before=L.s_xt)
            L.s_ppt = stage("p_t", 2, ["dve"], before=prev and prev.s_ppt)
            L.s_pg = stage("ple_gate", 8, ["act"], add=False, before=prev and prev.s_pg)
            L.s_pp = stage("ple_proj", 8, ["dve"], add=False, before=prev and prev.s_pp)
            for i in range(8):
                banks.add(L.s_pg, i)
                banks.add(L.s_pp, i)

        vec_in, x_in, h_done, out_done = sem("vec_in"), sem("x_in"), sem("h_done"), sem("out_done")
        consts = sem("consts")
        act_link, dve_link, pool_link = sem("act_link"), sem("dve_link"), sem("pool_link")
        sq_done, sqrt_done, xn_done = sem("sq_done"), sem("sqrt_done"), sem("xn_done")
        loaded = [sem(f"slot{n}_loaded") for n in range(NSLOT)]
        p_in = sem("p_in")
        soft_max_done, prob_done, prob_scaled = sem("row_max_done"), sem("prob_done"), sem("prob_scaled")
        lat_norm, rope_k, rope_q = sem("lat_norm"), sem("rope_k"), sem("rope_q")
        soft_e, soft_n = sem("router_exp"), sem("router_softmax")
        top_done, spread_done, onehot_done, gcol_done = sem("top_done"), sem("spread_done"), sem("onehot_done"), sem("gcol_done")
        gdn_in, alog_in = sem("w_ba_in"), sem("alog_in")
        conv_done, silu_q, sq16, rt_done, qk_done = (sem(x) for x in ("conv_done", "qkv_silu", "qk_squares", "qk_sqrt", "qk_scaled"))
        ba_exp, ba_dve, fac_done, masks = sem("ba_exp"), sem("ba_dve"), sem("factors"), sem("masks")
        gm_done, etm_done, ut_init, bv_done, kg_done, t0_done, r_done, o_done = (
            sem(x) for x in ("gm_done", "masked_decay", "ut_init", "bv_done", "kg_done", "t0_done", "rhs_done", "o_done"))
        o_norm, o_sqrt, gated = sem("o_norm"), sem("o_sqrt"), sem("gated")
        gdn_out1_in = sem("gdn_out1_in")
        fg_in = sem("fg_in")

        out_ready = sem("out_ready")

        block = ctx.enter_context(nc.Block())

        use = {}
        count = [0] * NSLOT

        def take(key, n):
            count[n] += 1
            use[key] = (loaded[n], 16 * count[n])

        for n, key in enumerate(["w_lat", "w_qb", "w_kvb", "w_mo0", "w_mo1"]):
            take(key, n)
        for l in range(2):
            lay[l].base = list(count)
            for n in range(NSLOT):
                count[n] += 6 * NE // NSLOT
            for n, key in enumerate([f"ple_g0{l}", f"ple_g1{l}", f"ple_p{l}"]):
                take(key, lay[l].rot + n)
            if l == 0:
                for u in range(8):
                    take(f"gdn_in{u}", 6 + u % 2)
                take("gdn_out0", 2)

        units = []
        for i in range(GRP):
            units += [("gate", i, 0), ("up", i, 0), ("gate", i, 1), ("up", i, 1)]
            if i:
                units += [("down", i - 1, 0), ("down", i - 1, 1)]
        units += [("down", GRP - 1, 0), ("down", GRP - 1, 1)]
        NU = len(units)
        unit_of = {u: n for n, u in enumerate(units)}
        expert_w = {"gate": moe_w_gate, "up": moe_w_up, "down": moe_w_down}

        def wait_use(eng, key):
            s, c = use[key]
            eng.wait_ge(s, c)

        norms = ["mix0", "ffn0", "ple0", "mix1", "ffn1", "ple1", "last"]
        norm_no = {n: i for i, n in enumerate(norms)}

        @block.sync
        def _(sp):
            for s, x in enumerate((x_prompt, x_sample)):
                sp.dma_start(h[:, NT * s:NT * s + NT, :],
                             x[0].rearrange("(j p) d -> p j d", p=P)).then_inc(x_in, 16)
            s0, _c = use["w_lat"]
            sp.dma_start(w_lat, mla_w_in[0].rearrange("(k p) n -> p k n", p=P)).then_inc(loaded[0], 16)
            sp.dma_start(w_qb, mla_w_qb[0].rearrange("(k p) n -> p k n", p=P)).then_inc(loaded[1], 16)
            sp.dma_start(w_kvb, mla_w_kvb[0]).then_inc(loaded[2], 16)
            wo = mla_w_out[0].rearrange("(k p) n -> p k n", p=P)
            for f in range(2):
                sp.dma_start(w_mo[f], wo[:, :, f * HALF:(f + 1) * HALF]).then_inc(loaded[3 + f], 16)

            def expert_unit(l, q, n, slot_n):
                kind, i, f = units[n]
                src = expert_w[kind][l].rearrange("e (k p) n -> e p k n", p=P)
                sp.dma_start(slot(slot_n, KD, HALF),
                             src[q * GRP + i, :, :, f * HALF:(f + 1) * HALF]).then_inc(loaded[slot_n], 16)

            def wait_unit_used(L, q, n):
                kind, i, f = units[n]
                if kind == "down":
                    sp.wait_ge(moe_sem["y_in_psum"], q * (2 * GRP) + (2 * i + f + 1) + L.done["y_in_psum"])
                else:
                    sp.wait_ge(moe_sem["gu_in_psum"], q * (4 * GRP) + (4 * i + 2 * f + (kind == "up") + 1) + L.done["gu_in_psum"])

            for l in LAYERS:
                if l == 1:
                    wi = gdn_w_in[0].rearrange("(k p) n -> p k n", p=P)
                    sp.dma_start(wba[:, :, :], wi[:, :, 4 * D:4 * D + 32]).then_inc(gdn_in, 16)
                    for u in range(8):
                        if u >= 2:
                            v = u - 2
                            sp.wait_ge(*(s_qkv.full(4 * v + 4) if v < 6 else s_z.full(4 * (v - 5))))
                        sp.dma_start(slot(6 + u % 2, KD, HALF), wi[:, :, u * HALF:(u + 1) * HALF]).then_inc(loaded[6 + u % 2], 16)
                    wo = gdn_w_out[0].rearrange("(k p) n -> p k n", p=P)
                    sp.wait_ge(*s_ba.full(1))
                    sp.dma_start(gw_out[1], wo[:, :, HALF:D]).then_inc(gdn_out1_in, 16)
                    sp.wait_ge(*s_vt.full(GH))
                    sp.dma_start(gw_out[0], wo[:, :, 0:HALF]).then_inc(loaded[2], 16)
                L = lay[l]
                if l == 0:
                    frees = [s_lat.full(NJ), s_qrt.full(4), s_sc.full(16), s_mo.full(8),
                             s_mo.full(8), s_sc.full(16), s_sc.full(16), s_ot.full(16)]
                    frees[1] = s_qr.full(NJ)
                else:
                    frees = [s_av.freed(15)] * NSLOT
                    frees[2] = s_go.full(8)
                    frees[5] = (gated, NJ)
                for n in range(NSLOT):
                    sp.wait_ge(*frees[(n + L.rot) % NSLOT])
                    expert_unit(l, 0, n, (n + L.rot) % NSLOT)
                with sp.Fori(0, NQ - 1) as q:
                    for n in range(NU):
                        wait_unit_used(L, q, n)
                        m = n + NSLOT
                        expert_unit(l, q + m // NU, m % NU, (m + L.rot) % NSLOT)
                for n in range((NQ - 1) * NU + NSLOT, NQ * NU):
                    wait_unit_used(L, NQ - 1, n % NU - NSLOT)
                    expert_unit(l, NQ - 1, n % NU, (n + L.rot) % NSLOT)
                wg = ple_w_gate[l].rearrange("(k p) n -> p k n", p=P)
                for f in range(2):
                    wait_unit_used(L, NQ - 1, NU - NSLOT + f)
                    sp.dma_start(slot(L.rot + f, KD, HALF), wg[:, :, f * HALF:(f + 1) * HALF]).then_inc(loaded[L.rot + f], 16)
                wait_unit_used(L, NQ - 1, NU - NSLOT + 2)
                sp.dma_start(slot(L.rot + 2, 2, D), ple_w_proj[l].rearrange("(k p) n -> p k n", p=P)).then_inc(loaded[L.rot + 2], 16)
                wait_unit_used(L, NQ - 1, NU - 1)
                for s, x in enumerate((p_prompt, p_sample)):
                    sp.dma_start(pin[:, NT * s:NT * s + NT, :],
                                 x[l, 0].rearrange("(j p) d -> p j d", p=P)).then_inc(p_in, 16)
                if l == 1:
                    sp.dma_start(fg, final_norm_g.partition_broadcast(P)).then_inc(fg_in, 16)
            sp.wait_ge(out_ready, 4)
            for s, y in enumerate((y_prompt, y_sample)):
                sp.dma_start(y[0].rearrange("(j p) d -> p j d", p=P),
                             xn[:, NT * s:NT * s + NT, :]).then_inc(out_done, 16)
            sp.wait_ge(out_done, 32)


        @block.gpsimd
        def _(pool):
            n = [0]

            def link(ins):
                n[0] += 1
                ins.then_inc(pool_link, 1)
                pool.wait_ge(pool_link, n[0])

            pool.dma_start(rows[ROW_MIX:ROW_MIX + 16, :], norm_mix_g.rearrange("l (k p) -> (l k) p", p=P)).then_inc(vec_in, 16)
            pool.dma_start(rows[ROW_FFN:ROW_FFN + 16, :], norm_ffn_g.rearrange("l (k p) -> (l k) p", p=P)).then_inc(vec_in, 16)
            pool.dma_start(rows[ROW_PLE:ROW_PLE + 16, :], norm_ple_g.rearrange("l (k p) -> (l k) p", p=P)).then_inc(vec_in, 16)
            pool.dma_start(rows[ROW_QN:ROW_QN + 2, :], mla_q_norm_g.rearrange("l (k p) -> (l k) p", p=P)).then_inc(vec_in, 16)
            pool.dma_start(rows[ROW_KVN:ROW_KVN + 1, :], mla_kv_norm_g).then_inc(vec_in, 16)
            pool.dma_start(cs[:, 0, :, :], rope_cos.rearrange("(j p) d -> p j d", p=P)).then_inc(vec_in, 16)
            pool.dma_start(cs[:, 1, :, :], rope_sin.rearrange("(j p) d -> p j d", p=P)).then_inc(vec_in, 16)
            for l in range(2):
                pool.dma_start(wr[:, l, :, :], moe_w_router[l].rearrange("(k p) n -> p k n", p=P)).then_inc(vec_in, 16)
            pool.dma_start(rows[ROW_GDN:ROW_GDN + 1, :], gdn_norm_g).then_inc(vec_in, 16)
            pool.dma_start(conv_rows, gdn_conv_w[0].rearrange("t (c p) -> (t c) p", p=P)).then_inc(vec_in, 16)
            pool.dma_start(alog[:, 0, :], gdn_A_log.rearrange("l d h -> (l d h)").partition_broadcast(P)).then_inc(alog_in, 16)
            pool.dma_start(alog[:, 1, :], gdn_dt_bias.rearrange("l d h -> (l d h)").partition_broadcast(P)).then_inc(alog_in, 16)
            link(pool.memset(ident[:, :], 0.0))
            link(pool.affine_select(out=ident[:, :], in_=ident[:, :], compare_op=ALU.not_equal, fill=1.0,
                                    base=0, pattern=[[-1, P]], channel_multiplier=1))
            link(pool.memset(diag32[:, :], 0.0))
            link(pool.affine_select(out=diag32[:, :], in_=diag32[:, :], compare_op=ALU.not_equal, fill=1.0,
                                    base=0, pattern=[[-1, 32]], channel_multiplier=1))
            link(pool.memset(ones[:, :], 1.0))
            link(pool.memset(eps[:, :], EPS))
            link(pool.memset(q_eps[:, :], EPS * P))
            link(pool.iota(token[:, :], pattern=[[P, NT]], base=0, channel_multiplier=1,
                           allow_small_or_imprecise_dtypes=True))
            link(pool.memset(tri[:, :, :], 1.0))
            for a, (cm, st, op) in enumerate(((-1, 1, ALU.is_ge), (1, -1, ALU.is_ge), (1, -1, ALU.is_gt), (-1, 1, ALU.is_gt))):
                link(pool.affine_select(out=tri[:, a, :], in_=tri[:, a, :], compare_op=op, fill=0.0, base=0,
                                        pattern=[[st, P]], channel_multiplier=cm))
            link(pool.iota(work[:, 0:P].bitcast(mybir.dt.int32), pattern=[[0, P]], base=0, channel_multiplier=1))
            link(pool.iota(work[:, P:2 * P].bitcast(mybir.dt.int32), pattern=[[1, P]], base=0, channel_multiplier=0))
            pool.sem_inc(consts, 1)
            def gdn_pool():
                pool.wait_ge(fac_done, 1)
                s_kt.wait_read(pool, GH - 1)
                s_vt.wait_read(pool, GH - 1)
                s_z.wait_read(pool, 7)
                for r, (d, f, m) in enumerate(rounds):
                    n = m if d == 0 else 1 - m
                    hs = slice(4 * f, 4 * f + 4)

                    def per_head(row, s):
                        return fac[:, row, NT * s + n, 8 * d + 4 * f:8 * d + 4 * f + 4].unsqueeze(2).to_broadcast([P, 4, P])

                    for s in range(NS):
                        if r:
                            pool.wait_ge(*core["decay"].full(gidx(r - 1, s) + 1))
                        pool.tensor_tensor(b_gm[s], tri[:, TRI_GT if d == 0 else TRI_LT, :].unsqueeze(1).to_broadcast([P, 4, P]),
                                           per_head(F_G, s), ALU.mult).then_inc(gm_done, 1)
                    for s in range(NS):
                        core["decay"].wait_read(pool, gidx(r, s))
                        if r:
                            pool.wait_ge(*core["av"].full(gidx(r - 1, s) + 1))
                        pool.tensor_tensor(b_at[s], tri[:, TRI_LE if d == 0 else TRI_GE, :].unsqueeze(1).to_broadcast([P, 4, P]),
                                           b_et[s], ALU.mult).then_inc(etm_done, 1)
                    for s in range(NS):
                        if r:
                            pool.wait_ge(*core["vn"].full(gidx(r - 1, s) + 1))
                        for b in (b_u[s], b_t[s]):
                            pool.tensor_copy(b, ident[:, :].unsqueeze(1).to_broadcast([P, 4, P])).then_inc(ut_init, 1)
                    for s in range(NS):
                        j = NT * s + n
                        pool.tensor_tensor(b_r[s], vnat[:, j, hs, :], per_head(F_BETA, s), ALU.mult).then_inc(bv_done, 1)
                        if m == 0:
                            if r:
                                pool.wait_ge(*core["st"].full(2 * (r // 2) - 2 + s + 1))
                            pool.tensor_tensor(b_kg[s], knat[:, j, hs, :], per_head(F_KG, s), ALU.mult).then_inc(kg_done, 1)

            for l in LAYERS:
                if l == 1:
                    gdn_pool()
                L = lay[l]
                L.s_st.wait_read(pool, 3)
                with pool.Fori(0, NQ) as q:
                    pool.wait_ge(moe_sem["scat_free"], q * 8 + 2 + L.done["scat_free"])
                    pool.wait_ge(consts, 1)
                    pool.tensor_copy(scs, sc[:, q, :, :]).then_inc(moe_sem["sc_staged"], 1)

        def norm_act(act, name, src, tag):
            i = norm_no[name]
            if i == 0:
                act.wait_ge(x_in, 32)
                act.wait_ge(masks, 1)
            else:
                act.wait_ge(h_done, i)
            for j in range(NJ):
                act.activation(work[:, :], h[:, j, :], ACT.Square,
                               accum_out=ss[:, j:j + 1]).then_inc(sq_done, 1)
                act.wait_ge(sq_done, 4 * i + j + 1)
            act.activation(rs[:, 0:NJ], ss[:, 0:NJ], ACT.Sqrt, bias=eps[:, :], scale=1.0 / D).then_inc(sqrt_done, 1)

        def xt_out(eng, which, st, row):
            for k in range(KD):
                if st.reader(k) != which:
                    continue
                eng.wait_ge(*st.full(k + 1))
                src, dst, g = psum[:, banks.bank(st, k), :], xt[:, k, :], gains[:, row + k:row + k + 1]
                if which == "act":
                    ins = eng.activation(dst, src, ACT.Copy, scale=g)
                else:
                    ins = eng.tensor_scalar(dst, src, g, None, ALU.mult)
                ins.then_inc(st.freed(k)[0], 1)

        @block.scalar
        def _(act):
            n = [0]

            def link(ins):
                n[0] += 1
                ins.then_inc(act_link, 1)
                act.wait_ge(act_link, n[0])

            def copy_out(st, i, dst, cols=HALF):
                act.wait_ge(*st.full(i + 1))
                act.activation(dst, psum[:, banks.bank(st, i), 0:cols], ACT.Copy).then_inc(st.freed(i)[0], 1)

            norm_act(act, "mix0", None, 0)
            s_vec.wait_read(act, 0)
            xt_out(act, "act", s_xt0, ROW_MIX)
            for j in range(0, NJ, 2):
                copy_out(s_lat, j, lat[:, j, :], LAT)
            s_lat.wait_read(act, NJ - 1)
            for j in range(NJ):
                link(act.activation(work[:, 0:QL], lat[:, j, 0:QL], ACT.Square, accum_out=ss[:, 4 + j:5 + j]))
                link(act.activation(work[:, 0:KVL], lat[:, j, QL:QL + KVL], ACT.Square, accum_out=ss[:, 8 + j:9 + j]))
            act.activation(rs[:, 4:8], ss[:, 4:8], ACT.Sqrt, bias=eps[:, :], scale=1.0 / QL).then_inc(sqrt_done, 1)
            act.activation(rs[:, 8:12], ss[:, 8:12], ACT.Sqrt, bias=eps[:, :], scale=1.0 / KVL).then_inc(sqrt_done, 1)
            for i in range(0, HEADS, 2):
                copy_out(s_qn, i, qt[:, i, :])
            for j in range(NJ):
                copy_out(s_qr, j, qrn[:, j, :])
            for i in range(0, HEADS, 2):
                copy_out(s_kn, i, kt[:, i, :])
            for i in range(0, 2 * NJ, 2):
                copy_out(s_v, i, vv[:, i // 2, 0:HALF])
            for i in range(18):
                if i < 16:
                    act.wait_ge(soft_max_done, i + 1)
                    if i >= 2:
                        act.wait_ge(*s_pt.full(i - 1))
                    b = banks.bank(s_sc, i)
                    for qh in range(2):
                        ins = act.activation(prob[:, i % 2, qh * SEQ:(qh + 1) * SEQ],
                                             psum[:, b, qh * SEQ:(qh + 1) * SEQ], ACT.Exp,
                                             bias=rs[:, 16 + 2 * (i % 2) + qh:17 + 2 * (i % 2) + qh], scale=SCALE,
                                             accum_out=ss[:, 16 + 2 * (i % 2) + qh:17 + 2 * (i % 2) + qh])
                        ins.then_inc(prob_done, 1)
                        if qh == 1:
                            act.wait_ge(prob_done, 2 * i + 2)
                            act.sem_inc(s_sc.freed(i)[0], 1)
                if i >= 2:
                    g = i - 2
                    s, hd = g // HEADS, g % HEADS
                    copy_out(s_ot, g, ot[:, hd, s * SEQ:(s + 1) * SEQ], SEQ)
            def gdn_act():
                norm_act(act, "mix1", None, 0)
                act.wait_ge(sq_done, 4 * norm_no["mix1"] + 4)
                xt_out(act, "act", s_xt1, ROW_MIX + 8)
                for c in range(25):
                    if c < 24:
                        act.wait_ge(*s_qkv.full(c + 1))
                        if c == 0:
                            act.wait_ge(masks, 2)
                        if c >= 2:
                            act.wait_ge(conv_done, c - 1)
                        act.activation(pad[:, c % 2, :, 2:258],
                                       psum[:, banks.bank(s_qkv, c), :].rearrange("p (s w) -> p s w", s=NS), ACT.Copy).then_inc(s_qkv.freed(c)[0], 1)
                    if c:
                        act.wait_ge(conv_done, c)
                        act.activation(qkv[:, c - 1, :].rearrange("p (s w) -> p s w", s=NS), cacc[:, (c - 1) % 2, :, :],
                                       ACT.Silu).then_inc(silu_q, 1)
                for i in range(8):
                    f, j = i // 4, i % 4
                    act.wait_ge(*s_z.full(i + 1))
                    act.activation(znat[:, j, 4 * f:4 * f + 4, :], psum[:, banks.bank(s_z, i), :].rearrange("p (h w) -> p h w", h=4),
                                   ACT.Silu).then_inc(s_z.freed(i)[0], 1)
                act.wait_ge(ba_dve, 1)
                act.activation(fac[:, F_X, :, :], fac[:, F_X, :, :], ACT.Exp, scale=-1.0).then_inc(ba_exp, 1)
                act.activation(fac[:, F_BETA, :, :], ba[:, :, 0:16], ACT.Exp, scale=-1.0).then_inc(ba_exp, 1)
                act.activation(alog[:, 0, :], alog[:, 0, :], ACT.Exp).then_inc(ba_exp, 1)
                act.wait_ge(ba_dve, 2)
                act.activation(fac[:, F_X, :, :], fac[:, F_X, :, :], ACT.Ln).then_inc(ba_exp, 1)
                act.wait_ge(*s_cum.full(1))
                cum = psum[:, banks.bank(s_cum, 0), 0:128].rearrange("p (a d j h) -> p a d j h", a=2, d=2, j=NJ)
                for d in range(2):
                    dh = slice(8 * d, 8 * d + 8)
                    act.activation(fac[:, F_EG, :, dh], cum[:, 0, d, :, :], ACT.Exp).then_inc(ba_exp, 1)
                    act.activation(fac[:, F_KG, :, dh], cum[:, 1, d, :, :], ACT.Exp).then_inc(ba_exp, 1)
                act.wait_ge(ba_exp, 8)
                act.sem_inc(s_cum.freed(0)[0], 1)
                for c in range(17):
                    if c < 16:
                        if c >= 2:
                            act.wait_ge(*s_nrm.full(c - 1))
                        if c == 0:
                            act.wait_ge(silu_q, 24)
                        act.activation(sqb[:, c % 2, :], qkv[:, c, :], ACT.Square).then_inc(sq16, 1)
                    if c:
                        k = c - 1
                        act.wait_ge(*s_nrm.full(k + 1))
                        if k >= 2:
                            act.wait_ge(qk_done, k - 1)
                        e, sc_ = (q_eps[:, :], float(P)) if k < GH else (eps[:, :], 1.0)
                        act.activation(rtb[:, k % 2, :], psum[:, banks.bank(s_nrm, k), :], ACT.Sqrt, bias=e, scale=sc_).then_inc(s_nrm.freed(k)[0], 1)
                for i in range(GH):
                    act.wait_ge(*s_kt.full(i + 1))
                    act.activation(knat[:, :, i, :], psum[:, banks.bank(s_kt, i), :].rearrange("p (j w) -> p j w", j=NJ),
                                   ACT.Copy).then_inc(s_kt.freed(i)[0], 1)

                def out(name, i, dst, func=ACT.Copy):
                    st = core[name]
                    act.wait_ge(*st.full(i + 1))
                    act.activation(dst, psum[:, banks.bank(st, i), :].rearrange("p (h w) -> p h w", h=4), func).then_inc(st.freed(i)[0], 1)

                s_z.wait_read(act, 7)
                for r, (d, f, m) in enumerate(rounds):
                    for s in range(NS):
                        if r:
                            core["kk"].wait_read(act, gidx(r - 1, s))
                            act.wait_ge(etm_done, gidx(r - 1, s) + 1)
                        out("decay", gidx(r, s), b_et[s], ACT.Exp)
                    for v in range(1, LEVELS):
                        for s in range(NS):
                            out("z", 12 * r + 2 * (v - 1) + s, b_z[s])
                    for s in range(NS):
                        out("vn", gidx(r, s), b_vn[s])
                    if m == 0:
                        for s in range(NS):
                            out("st", 2 * (r // 2) + s, b_s[s])
                act.wait_ge(o_norm, 1)
                act.activation(fac[:, F_Y, :, 0:8], fac[:, F_Y, :, 0:8], ACT.Sqrt, bias=eps[:, :], scale=1.0 / P).then_inc(o_sqrt, 1)
                for k in range(0, KD, 2):
                    act.wait_ge(*s_gt.full(k + 1))
                    act.activation(got[:, k, :], psum[:, banks.bank(s_gt, k), :], ACT.Copy,
                                   scale=gains[:, ROW_GDN:ROW_GDN + 1]).then_inc(s_gt.freed(k)[0], 1)

            for l in LAYERS:
                if l == 1:
                    gdn_act()
                L = lay[l]
                norm_act(act, f"ffn{l}", None, 0)
                xt_out(act, "act", L.s_xt, ROW_FFN + 8 * l)
                for j in range(NJ):
                    act.wait_ge(soft_n, 8 * l + 2 * j + 1)
                    act.activation(aff[:, j % NT, j // NT, :], work[:, 512 + 16 * j:528 + 16 * j], ACT.Exp,
                                   accum_out=ss[:, 20 + j:21 + j]).then_inc(soft_e, 1)
                for q in range(0, NQ, 2):
                    act.wait_ge(*L.s_st.full(q + 1))
                    act.activation(sc[:, q, :, :], psum[:, banks.bank(L.s_st, q), :], ACT.Copy).then_inc(L.s_st.freed(q)[0], 1)
                with act.Fori(0, NQ) as q:
                    for kp in range(2):
                        act.wait_ge(moe_sem["gather_in_psum"], q * 4 + (kp + 1) + L.done["gather_in_psum"])
                        for k in range(2):
                            src = psum[:, kp, k * 256:(k + 1) * 256].rearrange("p (s e c) -> p e s c", s=NS, e=GRP)
                            kk = 2 * kp + k
                            for s in range(NS):
                                act.activation(xe[:, kk, :, s, :], src[:, :, s, :], ACT.Copy,
                                               scale=gains[:, ROW_FFN + 8 * l + kk:ROW_FFN + 8 * l + kk + 1]).then_inc(moe_sem["gather_read_act"], 1)

                    def silu(i):
                        act.wait_ge(moe_sem["gu_in_psum"], q * (4 * GRP) + (4 * i + 4) + L.done["gu_in_psum"])
                        act.activation(sg[:, i % 2, :], psum[:, i % 2, :], ACT.Silu).then_inc(moe_sem["silu_done"], 1)

                    def y_out(i):
                        if i == 0:
                            act.wait_ge(moe_sem["scat_free"], q * 8 + 2 + L.done["scat_free"])
                            act.wait_ge(moe_sem["gate_staged"], q + 1 + L.done["gate_staged"])
                        for f in range(2):
                            act.wait_ge(moe_sem["y_in_psum"], q * 8 + (2 * i + f + 1) + L.done["y_in_psum"])
                            act.activation(ybuf[32 * i:32 * i + 32, 0, f * HALF:(f + 1) * HALF],
                                           psum[0:32, 4 + f, :], ACT.Copy,
                                           scale=gstep[0:32, i:i + 1]).then_inc(moe_sem["y_free_act"], 1)

                    silu(0)
                    for i in range(1, GRP):
                        silu(i)
                        y_out(i - 1)
                    y_out(GRP - 1)
                norm_act(act, f"ple{l}", None, 0)
                xt_out(act, "act", L.s_pxt, ROW_PLE + 8 * l)
                for i in range(8):
                    act.wait_ge(*L.s_pg.full(i + 1))
                    if i >= 2:
                        act.wait_ge(*L.s_pp.freed(i - 2))
                    act.activation(gate[:, i % 2, :], psum[:, banks.bank(L.s_pg, i), :],
                                   ACT.Sigmoid).then_inc(L.s_pg.freed(i)[0], 1)
            norm_act(act, "last", None, 0)

        @block.tensor
        def _(pe):
            def turn_xn(st):
                for k in range(KD):
                    banks.claim(pe, st, k)
                    for j in range(NJ):
                        mm = pe.transpose(psum[:, banks.bank(st, k), j * P:(j + 1) * P],
                                          xn[:, j, k * P:(k + 1) * P], ident[:, :])
                    mm.then_inc(st.filled, 1)

            def product(st, i, lhs, rhs, n, cols, last=True):
                banks.claim(pe, st, i)
                for k in range(n):
                    mm = pe.matmul(psum[:, banks.bank(st, i), 0:cols], lhs(k), rhs(k), start=(k == 0), stop=(k == n - 1))
                mm.then_inc(st.filled, 1)

            pe.wait_ge(consts, 1)
            pe.wait_ge(vec_in, 16 * 11)
            pe.transpose(psum[:, banks.bank(s_vec, 0), 0:NROWS], rows[0:NROWS, :], ident[0:NROWS, 0:NROWS]).then_inc(s_vec.filled, 1)
            pe.transpose(psum[:, banks.bank(s_vec, 1), 0:CONV * 24], conv_rows, ident[0:CONV * 24, 0:CONV * 24]).then_inc(s_vec.filled, 1)
            pe.wait_ge(xn_done, NJ)
            turn_xn(s_xt0)
            s_xt0.wait_read(pe, KD - 1)
            wait_use(pe, "w_lat")
            for j in range(NJ):
                product(s_lat, j, lambda k: xt[:, k, j * P:(j + 1) * P], lambda k: w_lat[:, k, :], KD, LAT)
            pe.wait_ge(lat_norm, 1)
            pe.wait_ge(rope_k, 1)
            for g in range(4):
                banks.claim(pe, s_lt, g)
                for j in range(NJ):
                    src = lat[:, j, g * P:(g + 1) * P] if g < 3 else krd[:, j, :]
                    mm = pe.transpose(psum[:, banks.bank(s_lt, g), j * P:(j + 1) * P], src, ident[:, :])
                mm.then_inc(s_lt.filled, 1)
            s_lt.wait_read(pe, 3)
            wait_use(pe, "w_qb")
            wq = w_qb.rearrange("p k (h w) -> p k h w", h=HEADS)
            for i in range(HEADS):
                product(s_qn, i, lambda k: wq[:, k, i, 0:NOPE], lambda k: qlt[:, k, :], 2, T)
            for j in range(NJ):
                product(s_qr, j, lambda k: qlt[:, k, j * P:(j + 1) * P], lambda k: wq[:, k, :, NOPE:NOPE + ROPE], 2, 512)
            wait_use(pe, "w_kvb")
            wkv = w_kvb.rearrange("p (h w) -> p h w", h=HEADS)
            for i in range(HEADS):
                product(s_kn, i, lambda k: wkv[:, i, 0:NOPE], lambda k: kvt, 1, T)
            for i in range(2 * NJ):
                j, f = i // 2, i % 2
                product(s_v, i, lambda k: kvt[:, j * P:(j + 1) * P], lambda k: wkv[:, 4 * f:4 * f + 4, NOPE:NOPE + DV], 1, HALF)
            pe.wait_ge(rope_q, 1)
            for g in range(4):
                banks.claim(pe, s_qrt, g)
                for j in range(NJ):
                    mm = pe.transpose(psum[:, banks.bank(s_qrt, g), j * P:(j + 1) * P], qrr[:, j, g * P:(g + 1) * P], ident[:, :])
                mm.then_inc(s_qrt.filled, 1)
            s_qn.wait_read(pe, HEADS - 1)
            s_kn.wait_read(pe, HEADS - 1)
            s_v.wait_read(pe, 2 * NJ - 1)
            s_qrt.wait_read(pe, 3)
            for i in range(18):
                if i < 16:
                    s, hd = i // HEADS, i % HEADS
                    banks.claim(pe, s_sc, i)
                    b = banks.bank(s_sc, i)
                    r0 = ROPE * (hd % 2)
                    keys = slice(s * SEQ, (s + 1) * SEQ)
                    for qh in range(2):
                        q0 = s * SEQ + qh * P
                        out = psum[:, b, qh * SEQ:(qh + 1) * SEQ]
                        pe.matmul(out, qt[:, hd, q0:q0 + P], kt[:, hd, keys], start=True, stop=False)
                        mm = pe.matmul(out, qrt[r0:r0 + ROPE, hd // 2, q0:q0 + P], krt[r0:r0 + ROPE, keys], start=False, stop=True)
                    mm.then_inc(s_sc.filled, 1)
                if 1 <= i < 17:
                    g = i - 1
                    pe.wait_ge(prob_scaled, g + 1)
                    banks.claim(pe, s_pt, g)
                    for kk in range(2):
                        for qh in range(2):
                            mm = pe.transpose(psum[:, banks.bank(s_pt, g), kk * SEQ + qh * P:kk * SEQ + (qh + 1) * P],
                                              prob[:, g % 2, qh * SEQ + kk * P:qh * SEQ + (kk + 1) * P], ident[:, :])
                    mm.then_inc(s_pt.filled, 1)
                if i >= 2:
                    g = i - 2
                    s, hd = g // HEADS, g % HEADS
                    s_pt.wait_read(pe, g)
                    product(s_ot, g, lambda k: vv[:, NT * s + k, hd * DV:(hd + 1) * DV],
                            lambda k: pt[:, g % 2, k * SEQ:(k + 1) * SEQ], 2, SEQ)
            s_ot.wait_read(pe, 15)
            for i in range(2 * NJ):
                j, f = i // 2, i % 2
                if i < 2:
                    wait_use(pe, f"w_mo{i}")
                product(s_mo, i, lambda k: ot[:, k, j * P:(j + 1) * P], lambda k: w_mo[f][:, k, :], HEADS, HALF)

            def gdn_pe():
                pe.wait_ge(xn_done, NJ * (norm_no["mix1"] + 1))
                turn_xn(s_xt1)
                s_xt1.wait_read(pe, KD - 1)
                for c in range(24):
                    if c % 4 == 0:
                        wait_use(pe, f"gdn_in{c // 4}")
                    w = slot(6 + (c // 4) % 2, KD, HALF)
                    product(s_qkv, c, lambda k: w[:, k, (c % 4) * P:(c % 4 + 1) * P], lambda k: xt[:, k, :], KD, T)
                for i in range(8):
                    f, j = i // 4, i % 4
                    if j == 0:
                        wait_use(pe, f"gdn_in{6 + f}")
                    product(s_z, i, lambda k: xt[:, k, j * P:(j + 1) * P], lambda k: slot(6 + f, KD, HALF)[:, k, :], KD, HALF)
                pe.wait_ge(gdn_in, 16)
                banks.claim(pe, s_ba, 0)
                for j in range(NJ):
                    for k in range(KD):
                        mm = pe.matmul(psum[:, banks.bank(s_ba, 0), 32 * j:32 * j + 32], xt[:, k, j * P:(j + 1) * P], wba[:, k, :],
                                       start=(k == 0), stop=(k == KD - 1))
                mm.then_inc(s_ba.filled, 1)
                pe.wait_ge(ba_dve, 3)
                banks.claim(pe, s_cum, 0)
                for a, masks_ in enumerate(((TRI_LE, TRI_GE), (TRI_GT, TRI_LT))):
                    for d in range(2):
                        c0 = 32 * (2 * a + d)
                        mm = pe.matmul(psum[:, banks.bank(s_cum, 0), c0:c0 + 32], tri[:, masks_[d], :], fac[:, F_G, :, 8 * d:8 * d + 8],
                                       start=True, stop=True)
                mm.then_inc(s_cum.filled, 1)
                for c in range(16):
                    pe.wait_ge(sq16, c + 1)
                    product(s_nrm, c, lambda k: ones[:, :], lambda k: sqb[:, c % 2, :], 1, T)
                for st, c0 in ((s_kt, GH), (s_vt, 2 * GH)):
                    if st is s_kt:
                        pe.wait_ge(qk_done, 16)
                    for i in range(GH):
                        banks.claim(pe, st, i)
                        for j in range(NJ):
                            mm = pe.transpose(psum[:, banks.bank(st, i), j * P:(j + 1) * P], qkv[:, c0 + i, j * P:(j + 1) * P], ident[:, :])
                        mm.then_inc(st.filled, 1)

                def four(name, i, lhs, rhs, turn=False):
                    st = core[name]
                    banks.claim(pe, st, i)
                    for g in range(4):
                        o = psum[:, banks.bank(st, i), g * P:(g + 1) * P]
                        mm = pe.transpose(o, lhs(g), ident[:, :]) if turn else pe.matmul(o, lhs(g), rhs(g), start=True, stop=True)
                    mm.then_inc(st.filled, 1)

                for r, (d, f, m) in enumerate(rounds):
                    n = m if d == 0 else 1 - m
                    tok = [slice((NT * s + n) * P, (NT * s + n + 1) * P) for s in range(NS)]
                    for s in range(NS):
                        pe.wait_ge(gm_done, gidx(r, s) + 1)
                        four("decay", gidx(r, s), lambda g: b_gm[s][:, g, :], lambda g: tri[:, TRI_LE if d == 0 else TRI_GE, :])
                    for s in range(NS):
                        four("kk", gidx(r, s), lambda g: qkv[:, GH + 4 * f + g, tok[s]], lambda g: qkv[:, GH + 4 * f + g, tok[s]])
                    for s in range(NS):
                        four("qk", gidx(r, s), lambda g: qkv[:, GH + 4 * f + g, tok[s]], lambda g: qkv[:, 4 * f + g, tok[s]])
                    for s in range(NS):
                        core["kk"].wait_read(pe, gidx(r, s))
                        four("lt", gidx(r, s), lambda g: b_lt[s][:, g, :], None, True)
                    for s in range(NS):
                        core["lt"].wait_read(pe, gidx(r, s))
                        four("n0", gidx(r, s), lambda g: b_n[s][:, g, :], None, True)
                    for v in range(1, LEVELS):
                        for s in range(NS):
                            if v == 1:
                                core["n0"].wait_read(pe, gidx(r, s))
                            else:
                                core["du"].wait_read(pe, 12 * r + 2 * (v - 2) + s)
                            four("z", 12 * r + 2 * (v - 1) + s, lambda g: b_n[s][:, g, :], lambda g: b_u[s][:, g, :])
                        for s in range(NS):
                            if v == 1:
                                pe.wait_ge(t0_done, gidx(r, s) + 1)
                            else:
                                core["dt"].wait_read(pe, 10 * r + 2 * (v - 2) + s)
                            core["z"].wait_read(pe, 12 * r + 2 * (v - 1) + s)
                            if v < LEVELS - 1:
                                four("dt", 10 * r + 2 * (v - 1) + s, lambda g: b_z[s][:, g, :], lambda g: b_t[s][:, g, :])
                            four("du", 12 * r + 2 * (v - 1) + s, lambda g: b_t[s][:, g, :], lambda g: b_z[s][:, g, :])
                    if m == 1:
                        for s in range(NS):
                            core["st"].wait_read(pe, 2 * (r // 2) + s)
                            four("ks", 2 * (r // 2) + s, lambda g: qkv[:, GH + 4 * f + g, tok[s]], lambda g: b_s[s][:, g, :])
                    for s in range(NS):
                        core["du"].wait_read(pe, 12 * r + 10 + s)
                        if m == 0:
                            pe.wait_ge(bv_done, gidx(r, s) + 1)
                        else:
                            pe.wait_ge(r_done, 2 * (r // 2) + s + 1)
                        four("vn", gidx(r, s), lambda g: b_u[s][:, g, :], lambda g: b_r[s][:, g, :])
                    if m == 1:
                        for s in range(NS):
                            four("qs", 2 * (r // 2) + s, lambda g: qkv[:, 4 * f + g, tok[s]], lambda g: b_s[s][:, g, :])
                    for s in range(NS):
                        core["vn"].wait_read(pe, gidx(r, s))
                        core["qk"].wait_read(pe, gidx(r, s))
                        four("av", gidx(r, s), lambda g: b_at[s][:, g, :], lambda g: b_vn[s][:, g, :])
                    if m == 0:
                        for s in range(NS):
                            pe.wait_ge(kg_done, 2 * (r // 2) + s + 1)
                            four("st", 2 * (r // 2) + s, lambda g: b_kg[s][:, g, :], lambda g: b_vn[s][:, g, :])
                for k in range(KD):
                    pe.wait_ge(gated, NJ)
                    banks.claim(pe, s_gt, k)
                    for j in range(NJ):
                        mm = pe.transpose(psum[:, banks.bank(s_gt, k), j * P:(j + 1) * P], o_acc[:, j, k, :], ident[:, :])
                    mm.then_inc(s_gt.filled, 1)
                s_gt.wait_read(pe, KD - 1)
                wait_use(pe, "gdn_out0")
                pe.wait_ge(gdn_out1_in, 16)
                for i in range(2 * NJ):
                    j, f = i // 2, i % 2
                    product(s_go, i, lambda k: got[:, k, j * P:(j + 1) * P], lambda k: gw_out[f][:, k, :], KD, HALF)

            for l in LAYERS:
                if l == 1:
                    gdn_pe()
                L = lay[l]
                pe.wait_ge(xn_done, NJ * (norm_no[f"ffn{l}"] + 1))
                turn_xn(L.s_xt)
                L.s_xt.wait_read(pe, KD - 1)
                for j in range(NJ):
                    product(L.s_lg, j, lambda k: xt[:, k, j * P:(j + 1) * P], lambda k: wr[:, l, k, :], KD, NE)
                pe.wait_ge(soft_n, 8 * l + 8)
                banks.claim(pe, L.s_at, 0)
                for t in range(NT):
                    mm = pe.transpose(psum[0:32, banks.bank(L.s_at, 0), t * P:(t + 1) * P],
                                      aff[:, t, :, :].rearrange("p s e -> p (s e)"), ident[:, :])
                mm.then_inc(L.s_at.filled, 1)
                pe.wait_ge(top_done, l + 1)
                banks.claim(pe, L.s_gt, 0)
                pe.transpose(psum[0:32, banks.bank(L.s_gt, 0), 0:32], topv[:, :], ident[0:32, 0:32]).then_inc(L.s_gt.filled, 1)
                pe.wait_ge(spread_done, l + 1)
                for s in range(NS):
                    product(L.s_ib, s, lambda k: ones[0:32, :], lambda k: spread[:, 16 * s:16 * s + 16, :], 1, HALF)
                pe.wait_ge(onehot_done, 4 * (l + 1))
                for q in range(NQ):
                    banks.claim(pe, L.s_st, q)
                    for j in range(NJ):
                        mm = pe.transpose(psum[:, banks.bank(L.s_st, q), j * P:(j + 1) * P],
                                          oh[:, j, q * P:(q + 1) * P], ident[:, :])
                    mm.then_inc(L.s_st.filled, 1)
                L.s_st.wait_read(pe, 3)
                pe.wait_ge(gcol_done, l + 1)
                with pe.Fori(0, NQ) as q:
                    pe.wait_ge(moe_sem["hid_free"], q * GRP + 2 + L.done["hid_free"])
                    for kp in range(4):
                        for k in range(2):
                            for s in range(NS):
                                o = psum[:, kp, k * 256 + s * P:k * 256 + (s + 1) * P]
                                c0 = (2 * kp + k) * P
                                for t in range(NT):
                                    mm = pe.matmul(o, xn[:, NT * s + t, c0:c0 + P], oh[:, NT * s + t, bass.ds(q * P, P)],
                                                   start=(t == 0), stop=(t == NT - 1))
                        mm.then_inc(moe_sem["gather_in_psum"], 1)
                    pe.wait_ge(moe_sem["gather_read_act"], (q + 1) * 8 + L.done["gather_read_act"])
                    pe.wait_ge(moe_sem["gather_read_dve"], (q + 1) * 8 + L.done["gather_read_dve"])

                    def wait_unit(kind, i, f):
                        m = unit_of[(kind, i, f)]
                        n = (m + L.rot) % NSLOT
                        pe.wait_ge(loaded[n], q * (16 * NU // NSLOT) + 16 * (L.base[n] + m // NSLOT + 1))
                        return slot(n, KD, HALF)

                    def gate_up(i):
                        pe.wait_ge(moe_sem["hid_free"], q * GRP + (i + 1) + L.done["hid_free"])
                        for f in range(2):
                            for b0, kind in ((0, "gate"), (2, "up")):
                                w = wait_unit(kind, i, f)
                                for ft in range(4):
                                    o = psum[:, b0 + i % 2, (4 * f + ft) * 64:(4 * f + ft + 1) * 64]
                                    for k in range(KD):
                                        mm = pe.matmul(o, w[:, k, ft * P:(ft + 1) * P], xe[:, k, i, :, :],
                                                       start=(k == 0), stop=(k == KD - 1))
                                mm.then_inc(moe_sem["gu_in_psum"], 1)

                    def down(i):
                        pe.wait_ge(moe_sem["hid_free"], q * GRP + (i + 3) + L.done["hid_free"])
                        for f in range(2):
                            w = wait_unit("down", i, f)
                            pe.wait_ge(moe_sem["y_free_act"], q * 8 + (2 * i + f + 1) + L.done["y_free_act"])
                            pe.wait_ge(moe_sem["y_free_dve"], q * 8 + (2 * i + f + 1) + L.done["y_free_dve"])
                            for k in range(KD):
                                mm = pe.matmul(psum[0:64, 4 + f, :], hid[:, i % 2, k * 64:(k + 1) * 64], w[:, k, :],
                                               start=(k == 0), stop=(k == KD - 1))
                            mm.then_inc(moe_sem["y_in_psum"], 1)

                    gate_up(0)
                    for i in range(1, GRP):
                        gate_up(i)
                        down(i - 1)
                    down(GRP - 1)
                    pe.wait_ge(moe_sem["sc_staged"], q + 1 + L.done["sc_staged"])
                    pe.wait_ge(moe_sem["y_free_act"], (q + 1) * 8 + 2 + L.done["y_free_act"])
                    pe.wait_ge(moe_sem["y_free_dve"], (q + 1) * 8 + 2 + L.done["y_free_dve"])
                    for g in range(8):
                        j, f = g // 2, g % 2
                        pe.wait_ge(moe_sem["scat_free"], q * 8 + (g + 1) + L.done["scat_free"])
                        pe.matmul(psum[:, 6 + g % 2, :], scs[:, j, :], ybuf[:, j // NT, f * HALF:(f + 1) * HALF],
                                  start=True, stop=True).then_inc(moe_sem["scat_in_psum"], 1)
                pe.wait_ge(xn_done, NJ * (norm_no[f"ple{l}"] + 1))
                turn_xn(L.s_pxt)
                pe.wait_ge(p_in, 32 * (l + 1))
                for k in range(2):
                    banks.claim(pe, L.s_ppt, k)
                    for j in range(NJ):
                        mm = pe.transpose(psum[:, banks.bank(L.s_ppt, k), j * P:(j + 1) * P], pin[:, j, k * P:(k + 1) * P], ident[:, :])
                    mm.then_inc(L.s_ppt.filled, 1)
                L.s_pxt.wait_read(pe, KD - 1)
                L.s_ppt.wait_read(pe, 1)
                for key in (f"ple_g0{l}", f"ple_g1{l}", f"ple_p{l}"):
                    wait_use(pe, key)
                wp = slot(L.rot + 2, 2, D)
                for i in range(8):
                    j, f = i // 2, i % 2
                    product(L.s_pg, i, lambda k: xt[:, k, j * P:(j + 1) * P], lambda k: slot(L.rot + f, KD, HALF)[:, k, :], KD, HALF)
                    product(L.s_pp, i, lambda k: ptt[:, k, j * P:(j + 1) * P], lambda k: wp[:, k, f * HALF:(f + 1) * HALF], 2, HALF)

        @block.vector
        def _(dve):
            n = [0]

            def link(ins):
                n[0] += 1
                ins.then_inc(dve_link, 1)
                dve.wait_ge(dve_link, n[0])

            def norm(name):
                i = norm_no[name]
                dve.wait_ge(sqrt_done, i + 1 + (2 if i else 0))
                link(dve.reciprocal(rs[:, 24:24 + NJ], rs[:, 0:NJ]))
                for j in range(NJ):
                    dve.tensor_scalar(xn[:, j, :], h[:, j, :], rs[:, 24 + j:25 + j], None, ALU.mult).then_inc(xn_done, 1)

            def copy_out(st, i, dst, cols=HALF):
                dve.wait_ge(*st.full(i + 1))
                dve.tensor_copy(dst, psum[:, banks.bank(st, i), 0:cols]).then_inc(st.freed(i)[0], 1)

            dve.wait_ge(*s_vec.full(1))
            dve.tensor_copy(gains[:, 0:NROWS], psum[:, banks.bank(s_vec, 0), 0:NROWS]).then_inc(s_vec.freed(0)[0], 1)
            dve.wait_ge(*s_vec.full(2))
            dve.tensor_copy(conv_w[:, :], psum[:, banks.bank(s_vec, 1), 0:CONV * 24]).then_inc(s_vec.freed(1)[0], 1)
            s_vec.wait_read(dve, 1)
            row, col, dif, sh = (work[:, a * P:(a + 1) * P].bitcast(mybir.dt.int32) for a in range(4))
            link(dve.tensor_tensor(dif, row, col, ALU.bitwise_xor))
            for v in range(LEVELS):
                link(dve.tensor_single_scalar(sh, dif, v, ALU.logical_shift_right))
                for side, m in enumerate((TRI_GT, TRI_LT)):
                    ins = dve.scalar_tensor_tensor(out=blocks[:, 2 * v + side, :], in0=sh, scalar=1.0, in1=tri[:, m, :],
                                                   op0=ALU.is_equal, op1=ALU.mult)
                    if side:
                        link(ins)
            dve.sem_inc(masks, 1)
            norm("mix0")
            xt_out(dve, "dve", s_xt0, ROW_MIX)
            for j in range(1, NJ, 2):
                copy_out(s_lat, j, lat[:, j, :], LAT)
            s_lat.wait_read(dve, NJ - 1)
            c4 = cs[:, 0, :, :]
            s4 = cs[:, 1, :, :]
            for s in range(NS):
                jj = slice(NT * s, NT * s + NT)
                x1, x2 = lat[:, jj, 384:416], lat[:, jj, 416:448]
                for d0 in (0, ROPE):
                    link(dve.tensor_tensor(rt1[:, jj, :], x1, c4, ALU.mult))
                    link(dve.tensor_tensor(rt2[:, jj, :], x2, s4, ALU.mult))
                    link(dve.tensor_tensor(krd[:, jj, d0:d0 + 32], rt1[:, jj, :], rt2[:, jj, :], ALU.subtract))
                    link(dve.tensor_tensor(rt1[:, jj, :], x2, c4, ALU.mult))
                    link(dve.tensor_tensor(rt2[:, jj, :], x1, s4, ALU.mult))
                    ins = dve.tensor_tensor(krd[:, jj, d0 + 32:d0 + 64], rt1[:, jj, :], rt2[:, jj, :], ALU.add)
                    if s == 1 and d0:
                        ins.then_inc(rope_k, 1)
                    else:
                        link(ins)
            dve.wait_ge(sqrt_done, 3)
            link(dve.reciprocal(rs[:, 4:12], rs[:, 4:12]))
            for j in range(NJ):
                link(dve.tensor_scalar(lat[:, j, 0:QL], lat[:, j, 0:QL], rs[:, 4 + j:5 + j], None, ALU.mult))
                ins = dve.tensor_scalar(lat[:, j, QL:QL + KVL], lat[:, j, QL:QL + KVL], rs[:, 8 + j:9 + j], None, ALU.mult)
                if j < NJ - 1:
                    link(ins)
                else:
                    ins.then_inc(lat_norm, 1)
            for g in range(4):
                dve.wait_ge(*s_lt.full(g + 1))
                dst = qlt[:, g, :] if g < 2 else (kvt if g == 2 else krt)
                src = psum[:, banks.bank(s_lt, g), :]
                if g < 3:
                    dve.tensor_scalar(dst, src, gains[:, ROW_QN + g:ROW_QN + g + 1], None, ALU.mult).then_inc(s_lt.freed(g)[0], 1)
                else:
                    dve.tensor_copy(dst, src).then_inc(s_lt.freed(g)[0], 1)
            for i in range(1, HEADS, 2):
                copy_out(s_qn, i, qt[:, i, :])
            for j in range(NJ):
                s_qr.wait_read(dve, j)
                v = qrn[:, j, :].rearrange("p (h w) -> p h w", h=HEADS)
                o = qrr[:, j, :].rearrange("p (h w) -> p h w", h=HEADS)
                cb = cs[:, 0, j % NT, :].unsqueeze(1).to_broadcast([P, HEADS, 32])
                sb_ = cs[:, 1, j % NT, :].unsqueeze(1).to_broadcast([P, HEADS, 32])
                w1 = work[:, 0:256].rearrange("p (h w) -> p h w", h=HEADS)
                w2 = work[:, 256:512].rearrange("p (h w) -> p h w", h=HEADS)
                w3 = work[:, 512:768].rearrange("p (h w) -> p h w", h=HEADS)
                w4 = work[:, 768:1024].rearrange("p (h w) -> p h w", h=HEADS)
                dve.tensor_tensor(w1, v[:, :, 0:32], cb, ALU.mult)
                dve.tensor_tensor(w2, v[:, :, 32:64], sb_, ALU.mult)
                dve.tensor_tensor(w3, v[:, :, 32:64], cb, ALU.mult)
                link(dve.tensor_tensor(w4, v[:, :, 0:32], sb_, ALU.mult))
                dve.tensor_tensor(o[:, :, 0:32], w1, w2, ALU.subtract)
                ins = dve.tensor_tensor(o[:, :, 32:64], w3, w4, ALU.add)
                if j < NJ - 1:
                    link(ins)
                else:
                    ins.then_inc(rope_q, 1)
            for i in range(1, HEADS, 2):
                copy_out(s_kn, i, kt[:, i, :])
            for i in range(1, 2 * NJ, 2):
                copy_out(s_v, i, vv[:, i // 2, HALF:D])
            for g in range(4):
                copy_out(s_qrt, g, qrt[:, g, :])
            for i in range(17):
                if i < 16:
                    b = i % 2
                    dve.wait_ge(*s_sc.full(i + 1))
                    if i >= 2:
                        dve.wait_ge(prob_done, 2 * i - 2)
                    link(dve.tensor_reduce(rs[:, 20 + 2 * b:22 + 2 * b],
                                           psum[:, banks.bank(s_sc, i), :].rearrange("p (a k) -> p a k", a=2),
                                           AX_X, ALU.max))
                    dve.tensor_scalar(rs[:, 16 + 2 * b:18 + 2 * b], rs[:, 20 + 2 * b:22 + 2 * b], -SCALE, None,
                                      ALU.mult).then_inc(soft_max_done, 1)
                if i >= 1:
                    g = i - 1
                    if g >= 1:
                        dve.wait_ge(*s_pt.full(g))
                        if g >= 3:
                            dve.wait_ge(*s_ot.full(g - 2))
                        dve.tensor_copy(pt[:, (g - 1) % 2, :], psum[:, banks.bank(s_pt, g - 1), :]).then_inc(s_pt.freed(g - 1)[0], 1)
                    b = g % 2
                    dve.wait_ge(prob_done, 2 * g + 2)
                    link(dve.reciprocal(ss[:, 24 + 2 * b:26 + 2 * b], ss[:, 16 + 2 * b:18 + 2 * b]))
                    for qh in range(2):
                        ins = dve.tensor_scalar(prob[:, b, qh * SEQ:(qh + 1) * SEQ], prob[:, b, qh * SEQ:(qh + 1) * SEQ],
                                                ss[:, 24 + 2 * b + qh:25 + 2 * b + qh], None, ALU.mult)
                        if qh:
                            ins.then_inc(prob_scaled, 1)
            copy_out(s_pt, 15, pt[:, 1, :])
            for i in range(2 * NJ):
                j, f = i // 2, i % 2
                dve.wait_ge(*s_mo.full(i + 1))
                hv = h[:, j, f * HALF:(f + 1) * HALF]
                dve.tensor_tensor(hv, hv, psum[:, banks.bank(s_mo, i), :], ALU.add).then_inc(s_mo.freed(i)[0], 1)
            s_mo.wait_read(dve, 2 * NJ - 1)
            dve.sem_inc(h_done, 1)

            def gdn_dve():
                norm("mix1")
                xt_out(dve, "dve", s_xt1, ROW_MIX + 8)
                link(dve.memset(pad[:, :, :, 0:2], 0.0))
                dve.memset(pad[:, :, :, 258:260], 0.0).then_inc(masks, 1)
                for c in range(24):
                    s_qkv.wait_read(dve, c)
                    if c >= 2:
                        dve.wait_ge(silu_q, c - 1)
                    a = cacc[:, c % 2, :, :]
                    for t in range(CONV):
                        x = pad[:, c % 2, :, t:t + SEQ]
                        w = conv_w[:, 24 * t + c:24 * t + c + 1]
                        if t == 0:
                            ins = dve.tensor_scalar(a, x, w, None, ALU.mult)
                        else:
                            ins = dve.scalar_tensor_tensor(out=a, in0=x, scalar=w, in1=a, op0=ALU.mult, op1=ALU.add)
                        if t < CONV - 1:
                            link(ins)
                        else:
                            ins.then_inc(conv_done, 1)
                dve.wait_ge(*s_ba.full(1))
                dve.tensor_copy(ba[:, :, :], psum[:, banks.bank(s_ba, 0), 0:128].rearrange("p (j w) -> p j w", j=NJ)).then_inc(s_ba.freed(0)[0], 1)
                s_ba.wait_read(dve, 0)
                dve.wait_ge(alog_in, 32)
                x, y = fac[:, F_X, :, :], fac[:, F_Y, :, :]
                link(dve.tensor_tensor(y, ba[:, :, 16:32], alog[:, 1, :].unsqueeze(1).to_broadcast([P, NJ, 16]), ALU.add))
                dve.scalar_tensor_tensor(out=x, in0=y, scalar=-1.0, in1=y, op0=ALU.mult, op1=ALU.max).then_inc(ba_dve, 1)

                def scale_qk():
                    for c in range(16):
                        s_nrm.wait_read(dve, c)
                        link(dve.reciprocal(rtb[:, c % 2, :], rtb[:, c % 2, :]))
                        dve.tensor_tensor(qkv[:, c, :], qkv[:, c, :], rtb[:, c % 2, :], ALU.mult).then_inc(qk_done, 1)

                dve.wait_ge(ba_exp, 3)
                b, nb = fac[:, F_BETA, :, :], fac[:, F_NBETA, :, :]
                link(dve.tensor_scalar(b, b, 1.0, None, ALU.add))
                link(dve.reciprocal(b, b))
                link(dve.tensor_scalar(nb, b, -1.0, None, ALU.mult))
                dve.tensor_scalar(x, x, 1.0, None, ALU.add).then_inc(ba_dve, 1)
                dve.wait_ge(ba_exp, 4)
                link(dve.scalar_tensor_tensor(out=x, in0=y, scalar=0.0, in1=x, op0=ALU.max, op1=ALU.add))
                link(dve.tensor_scalar(x, x, -1.0, None, ALU.mult))
                dve.tensor_tensor(fac[:, F_G, :, :], x, alog[:, 0, :].unsqueeze(1).to_broadcast([P, NJ, 16]), ALU.mult).then_inc(ba_dve, 1)
                dve.wait_ge(ba_exp, 8)
                dve.tensor_tensor(fac[:, F_BEG, :, :], fac[:, F_EG, :, :], b, ALU.mult).then_inc(fac_done, 1)
                scale_qk()
                for i in range(GH):
                    dve.wait_ge(*s_vt.full(i + 1))
                    dve.tensor_copy(vnat[:, :, i, :], psum[:, banks.bank(s_vt, i), :].rearrange("p (j w) -> p j w", j=NJ)).then_inc(s_vt.freed(i)[0], 1)

                def bank4(name, i):
                    dve.wait_ge(core[name].filled, i + 1)
                    return psum[:, banks.bank(core[name], i), :].rearrange("p (h w) -> p h w", h=4)

                def done(name, i, ins):
                    ins.then_inc(core[name].freed(i)[0], 1)

                for r, (d, f, m) in enumerate(rounds):
                    n = m if d == 0 else 1 - m
                    hs = slice(4 * f, 4 * f + 4)

                    def per_head(row, s):
                        return fac[:, row, NT * s + n, 8 * d + 4 * f:8 * d + 4 * f + 4].unsqueeze(2).to_broadcast([P, 4, P])

                    def block(v, turned):
                        side = (d + turned) % 2
                        return blocks[:, 2 * v + side, :].unsqueeze(1).to_broadcast([P, 4, P])

                    for s in range(NS):
                        i = gidx(r, s)
                        core["decay"].wait_read(dve, i)
                        done("kk", i, dve.tensor_tensor(b_lt[s], b_et[s], bank4("kk", i), ALU.mult))
                    for s in range(NS):
                        i = gidx(r, s)
                        dve.wait_ge(etm_done, i + 1)
                        done("qk", i, dve.tensor_tensor(b_at[s], b_at[s], bank4("qk", i), ALU.mult))
                    for s in range(NS):
                        i = gidx(r, s)
                        done("lt", i, dve.tensor_tensor(b_n[s], per_head(F_NBETA, s), bank4("lt", i), ALU.mult))
                    for s in range(NS):
                        i = gidx(r, s)
                        dve.wait_ge(ut_init, 4 * r + 2 * s + 2)
                        core["lt"].wait_read(dve, i)
                        done("n0", i, dve.copy_predicated(b_u[s], block(0, 1), bank4("n0", i)))
                        dve.copy_predicated(b_t[s], block(0, 0), b_n[s]).then_inc(t0_done, 1)
                    for v in range(1, LEVELS):
                        for s in range(NS):
                            i, k = 12 * r + 2 * (v - 1) + s, 10 * r + 2 * (v - 1) + s
                            du = bank4("du", i)
                            core["n0"].wait_read(dve, gidx(r, s)) if v == 1 else core["du"].wait_read(dve, i - 2)
                            done("du", i, dve.copy_predicated(b_u[s], block(v, 1), du))
                            if v < LEVELS - 1:
                                dve.wait_ge(t0_done, gidx(r, s) + 1) if v == 1 else core["dt"].wait_read(dve, k - 2)
                                done("dt", k, dve.copy_predicated(b_t[s], block(v, 0), bank4("dt", k)))
                    if m == 1:
                        for s in range(NS):
                            i = 2 * (r // 2) + s
                            dve.wait_ge(bv_done, gidx(r, s) + 1)
                            done("ks", i, dve.tensor_tensor(b_tmp[s], per_head(F_BEG, s), bank4("ks", i), ALU.mult))
                            core["ks"].wait_read(dve, i)
                            dve.tensor_tensor(b_r[s], b_r[s], b_tmp[s], ALU.subtract).then_inc(r_done, 1)
                        for s in range(NS):
                            i = 2 * (r // 2) + s
                            dve.wait_ge(r_done, i + 1)
                            done("qs", i, dve.tensor_tensor(b_tmp[s], per_head(F_EG, s), bank4("qs", i), ALU.mult))
                    for s in range(NS):
                        i = gidx(r, s)
                        o = o_acc[:, NT * s + n, hs, :]
                        if m == 1:
                            core["qs"].wait_read(dve, 2 * (r // 2) + s)
                            if d == 1:
                                link(dve.tensor_tensor(b_tmp[s], b_tmp[s], o, ALU.add))
                            done("av", i, dve.tensor_tensor(o, b_tmp[s], bank4("av", i), ALU.add))
                        elif d == 1:
                            done("av", i, dve.tensor_tensor(o, o, bank4("av", i), ALU.add))
                        else:
                            done("av", i, dve.tensor_copy(o, bank4("av", i)))
                core["av"].wait_read(dve, 15)
                for j in range(NJ):
                    link(dve.tensor_tensor(b_n_sq, o_acc[:, j, :, :], o_acc[:, j, :, :], ALU.mult))
                    ins = dve.tensor_reduce(fac[:, F_Y, j, 0:8], b_n_sq, AX_X, ALU.add)
                    if j < NJ - 1:
                        link(ins)
                    else:
                        ins.then_inc(o_norm, 1)
                dve.wait_ge(o_sqrt, 1)
                link(dve.reciprocal(fac[:, F_Y, :, 0:8], fac[:, F_Y, :, 0:8]))
                for j in range(NJ):
                    o = o_acc[:, j, :, :]
                    link(dve.tensor_tensor(o, o, fac[:, F_Y, j, 0:8].unsqueeze(2).to_broadcast([P, GH, P]), ALU.mult))
                    dve.tensor_tensor(o, o, znat[:, j, :, :], ALU.mult).then_inc(gated, 1)
                for k in range(1, KD, 2):
                    dve.wait_ge(*s_gt.full(k + 1))
                    dve.tensor_scalar(got[:, k, :], psum[:, banks.bank(s_gt, k), :], gains[:, ROW_GDN:ROW_GDN + 1], None,
                                      ALU.mult).then_inc(s_gt.freed(k)[0], 1)
                for i in range(2 * NJ):
                    j, f = i // 2, i % 2
                    dve.wait_ge(*s_go.full(i + 1))
                    hv = h[:, j, f * HALF:(f + 1) * HALF]
                    dve.tensor_tensor(hv, hv, psum[:, banks.bank(s_go, i), :], ALU.add).then_inc(s_go.freed(i)[0], 1)
                s_go.wait_read(dve, 2 * NJ - 1)
                dve.sem_inc(h_done, 1)

            for l in LAYERS:
                if l == 1:
                    gdn_dve()
                L = lay[l]
                norm(f"ffn{l}")
                xt_out(dve, "dve", L.s_xt, ROW_FFN + 8 * l)
                for j in range(NJ):
                    dve.wait_ge(*L.s_lg.full(j + 1))
                    lg = psum[:, banks.bank(L.s_lg, j), 0:NE]
                    link(dve.tensor_reduce(rs[:, 12:13], lg, AX_X, ALU.max))
                    dve.tensor_scalar(work[:, 512 + 16 * j:528 + 16 * j], lg, rs[:, 12:13], None, ALU.subtract).then_inc(soft_n, 1)
                    dve.wait_ge(soft_e, 4 * l + j + 1)
                    dve.sem_inc(L.s_lg.freed(j)[0], 1)
                    link(dve.reciprocal(rs[:, 13:14], ss[:, 20 + j:21 + j]))
                    a = aff[:, j % NT, j // NT, :]
                    dve.tensor_scalar(a, a, rs[:, 13:14], None, ALU.mult).then_inc(soft_n, 1)
                dve.wait_ge(*L.s_at.full(1))
                dve.tensor_copy(afft, psum[0:32, banks.bank(L.s_at, 0), 0:SEQ]).then_inc(L.s_at.freed(0)[0], 1)
                L.s_at.wait_read(dve, 0)
                for r in range(CAP // 8):
                    v8, i8 = topv[:, 8 * r:8 * r + 8], topi[:, 8 * r:8 * r + 8]
                    link(dve.max(v8, afft))
                    link(dve.max_index(i8, v8, afft))
                    if r < CAP // 8 - 1:
                        link(dve.match_replace(afft, v8, afft, -1.0))
                dve.tensor_copy(topf[:, :], topi[:, :]).then_inc(top_done, 1)
                dve.wait_ge(top_done, l + 1)
                dve.tensor_tensor(spread, topf[:, :].unsqueeze(1).to_broadcast([32, 32, CAP]),
                                  diag32[:, :].unsqueeze(2).to_broadcast([32, 32, CAP]), ALU.mult).then_inc(spread_done, 1)
                dve.wait_ge(*L.s_gt.full(1))
                g0 = psum[0:32, banks.bank(L.s_gt, 0), :]
                dve.tensor_copy(gcol[0:32, :], g0[:, 0:NE])
                link(dve.tensor_copy(gcol[32:64, :], g0[:, NE:2 * NE]))
                dve.sem_inc(L.s_gt.freed(0)[0], 1)
                dve.sem_inc(gcol_done, 1)
                for s in range(NS):
                    dve.wait_ge(*L.s_ib.full(s + 1))
                    for t in range(NT):
                        dve.tensor_scalar(oh[:, NT * s + t, :], psum[:, banks.bank(L.s_ib, s), :],
                                          token[:, t:t + 1], None, ALU.is_equal).then_inc(onehot_done, 1)
                    dve.wait_ge(onehot_done, 4 * l + 2 * s + 2)
                    dve.sem_inc(L.s_ib.freed(s)[0], 1)
                for q in range(1, NQ, 2):
                    dve.wait_ge(*L.s_st.full(q + 1))
                    dve.tensor_copy(sc[:, q, :, :], psum[:, banks.bank(L.s_st, q), :]).then_inc(L.s_st.freed(q)[0], 1)
                if l == 0:
                    for name in ("hid_free", "y_free_act", "y_free_dve", "scat_free"):
                        dve.sem_inc(moe_sem[name], 2)
                with dve.Fori(0, NQ) as q:
                    dve.wait_ge(moe_sem["y_free_act"], q * 8 + 2 + L.done["y_free_act"])
                    dve.tensor_scalar(gstep[:, :], gcol[:, bass.ds(q * GRP, GRP)], 1.0, None, ALU.mult).then_inc(moe_sem["gate_staged"], 1)
                    for kp in range(2, 4):
                        dve.wait_ge(moe_sem["gather_in_psum"], q * 4 + (kp + 1) + L.done["gather_in_psum"])
                        for k in range(2):
                            src = psum[:, kp, k * 256:(k + 1) * 256].rearrange("p (s e c) -> p e s c", s=NS, e=GRP)
                            kk = 2 * kp + k
                            for s in range(NS):
                                dve.tensor_scalar(xe[:, kk, :, s, :], src[:, :, s, :],
                                                  gains[:, ROW_FFN + 8 * l + kk:ROW_FFN + 8 * l + kk + 1], None,
                                                  ALU.mult).then_inc(moe_sem["gather_read_dve"], 1)

                    def hidden(i):
                        dve.wait_ge(moe_sem["silu_done"], q * GRP + (i + 1) + L.done["silu_done"])
                        dve.tensor_tensor(hid[:, i % 2, :], sg[:, i % 2, :], psum[:, 2 + i % 2, :], ALU.mult).then_inc(moe_sem["hid_free"], 1)

                    def y_out(i):
                        if i == 0:
                            dve.wait_ge(moe_sem["gate_staged"], q + 1 + L.done["gate_staged"])
                        for f in range(2):
                            dve.wait_ge(moe_sem["y_in_psum"], q * 8 + (2 * i + f + 1) + L.done["y_in_psum"])
                            dve.tensor_scalar(ybuf[32 * i:32 * i + 32, 1, f * HALF:(f + 1) * HALF],
                                              psum[32:64, 4 + f, :], gstep[32:64, i:i + 1], None,
                                              ALU.mult).then_inc(moe_sem["y_free_dve"], 1)

                    hidden(0)
                    for i in range(1, GRP):
                        hidden(i)
                        y_out(i - 1)
                    y_out(GRP - 1)
                    for g in range(8):
                        j, f = g // 2, g % 2
                        dve.wait_ge(moe_sem["scat_in_psum"], q * 8 + (g + 1) + L.done["scat_in_psum"])
                        hv = h[:, j, f * HALF:(f + 1) * HALF]
                        dve.tensor_tensor(hv, hv, psum[:, 6 + g % 2, :], ALU.add).then_inc(moe_sem["scat_free"], 1)
                dve.wait_ge(moe_sem["scat_free"], 8 * NQ + 2 + L.done["scat_free"])
                dve.sem_inc(h_done, 1)
                norm(f"ple{l}")
                xt_out(dve, "dve", L.s_pxt, ROW_PLE + 8 * l)
                for k in range(2):
                    copy_out(L.s_ppt, k, ptt[:, k, :])
                for i in range(8):
                    j, f = i // 2, i % 2
                    dve.wait_ge(*L.s_pg.freed(i))
                    dve.wait_ge(*L.s_pp.full(i + 1))
                    dve.tensor_tensor(prod[:, i % 2, :], gate[:, i % 2, :], psum[:, banks.bank(L.s_pp, i), :],
                                      ALU.mult).then_inc(L.s_pp.freed(i)[0], 1)
                    dve.wait_ge(*L.s_pp.freed(i))
                    hv = h[:, j, f * HALF:(f + 1) * HALF]
                    link(dve.tensor_tensor(hv, hv, prod[:, i % 2, :], ALU.add))
                dve.sem_inc(h_done, 1)
            norm("last")
            dve.wait_ge(fg_in, 16)
            dve.wait_ge(xn_done, NJ * len(norms))
            for j in range(NJ):
                dve.tensor_tensor(xn[:, j, :], xn[:, j, :], fg, ALU.mult).then_inc(out_ready, 1)


_ORDER = ['x_prompt', 'x_sample', 'p_prompt', 'p_sample', 'norm_mix_g', 'norm_ffn_g', 'norm_ple_g',
          'final_norm_g', 'mla_w_in', 'mla_q_norm_g', 'mla_w_qb', 'mla_kv_norm_g', 'mla_w_kvb', 'mla_w_out',
          'gdn_w_in', 'gdn_conv_w', 'gdn_A_log', 'gdn_dt_bias', 'gdn_norm_g', 'gdn_w_out',
          'moe_w_router', 'moe_w_gate', 'moe_w_up', 'moe_w_down', 'ple_w_proj', 'ple_w_gate']


def kernel(**inputs):
    import concourse.bacc as _bacc
    from concourse.bass_utils import run_bass_kernel_spmd as _run

    inv = 10000.0 ** (-np.arange(0, ROPE, 2, dtype=np.float32) / ROPE)
    ang = np.arange(SEQ, dtype=np.float32)[:, None] * inv[None, :].astype(np.float32)
    tables = {"rope_cos": np.cos(ang).astype(np.float32), "rope_sin": np.sin(ang).astype(np.float32)}
    nc = _bacc.Bacc("TRN2", target_bir_lowering=False, num_devices=1, dynamic_dma_scratch_size=4096)
    arrays, args = {}, []
    for name in _ORDER + list(tables):
        a = tables[name] if name in tables else np.ascontiguousarray(inputs[name])
        arrays[f"in_{name}"] = a
        args.append(nc.dram_tensor(f"in_{name}", a.shape, mybir.dt.from_np(a.dtype), kind="ExternalInput").ap())
    for name in ("y_prompt", "y_sample"):
        args.append(nc.dram_tensor(f"out_{name}", (1, SEQ, D), F32, kind="ExternalOutput").ap())
    trunk_kernel(nc, *args)
    r = _run(nc, [arrays], core_ids=[0])
    return r.results[0]["out_y_prompt"], r.results[0]["out_y_sample"]
```

```python
from contextlib import ExitStack

import numpy as np

import concourse.bass as bass
from concourse import mybir

P = 128
F32 = mybir.dt.float32
F32R = mybir.dt.float32r
U32 = mybir.dt.uint32
ALU = mybir.AluOpType
ACT = mybir.ActivationFunctionType
AX_X = mybir.AxisListType.X

D = 1024
KD = D // P
NS = 2
SEQ = 256
T = NS * SEQ
NJ = T // P
NT = SEQ // P
EPS = 1e-6
HEADS = 8
NOPE, ROPE, DV = 128, 64, 128
QL, KVL = 256, 128
LAT = QL + KVL + ROPE
SCALE = (NOPE + ROPE) ** -0.5
PLE = 256
NE = 16
FE = 1024
CAP = 2 * SEQ // NE
NSLOT = 8
SLOTW = 4096
HALF = 512
GRP = 4
NQ = NE // GRP
NRAW = 4
NSPL = 3
QW = HALF // 2
NTOK = NS * CAP
POOL_HALVES = (("gate", 0), ("up", 1), ("down", 0))
LAYERS = range(2)
NBANK = 8

ROW_MIX, ROW_FFN, ROW_PLE, ROW_QN, ROW_KVN = 0, 16, 32, 48, 50
ROW_GDN = 51
NROWS = 52

GH = 8
CONV = 5
GQKV = 3 * D
LEVELS = 7
TRI_LE, TRI_GE, TRI_GT, TRI_LT = range(4)
F_G, F_BETA, F_NBETA, F_EG, F_BEG, F_KG, F_X, F_Y = range(8)


class Stage:

    def __init__(self, sem, name, n, readers, before=None):
        self.name, self.n, self.readers = name, n, readers
        self.filled = before.filled if before else sem(name + "_in_psum")
        self.read = before.read if before else {r: sem(f"{name}_read_{r}") for r in dict.fromkeys(readers)}
        self.past = before.past + before.n if before else 0
        self.past_read = {r: before.freed(max(i for i in range(before.n) if before.reader(i) == r))[1] if before else 0
                          for r in self.read}
        self.at = {}

    def full(self, count):
        return self.filled, self.past + count

    def reader(self, i):
        return self.readers[i % len(self.readers)]

    def freed(self, i):
        r = self.reader(i)
        per = self.readers.count(r)
        before = [x for x in range(i % len(self.readers)) if self.readers[x] == r]
        return self.read[r], self.past_read[r] + (i // len(self.readers)) * per + len(before) + 1

    def wait_read(self, eng, upto):
        need = {}
        for i in range(max(0, upto + 1 - len(self.readers)), upto + 1):
            s, c = self.freed(i)
            need[self.reader(i)] = (s, c)
        for s, c in need.values():
            eng.wait_ge(s, c)


class Ring:

    def __init__(self):
        self.order = []

    def add(self, stage, i):
        stage.at[i] = len(self.order)
        self.order.append((stage, i))

    def bank(self, stage, i):
        return stage.at[i] % NBANK

    def claim(self, pe, stage, i):
        at = stage.at[i] - NBANK
        if at >= 0:
            before, n = self.order[at]
            s, c = before.freed(n)
            pe.wait_ge(s, c)


def trunk_kernel(nc, x_prompt, x_sample, p_prompt, p_sample, norm_mix_g, norm_ffn_g, norm_ple_g,
                 final_norm_g, mla_w_in, mla_q_norm_g, mla_w_qb, mla_kv_norm_g, mla_w_kvb, mla_w_out,
                 gdn_w_in, gdn_conv_w, gdn_A_log, gdn_dt_bias, gdn_norm_g, gdn_w_out,
                 moe_w_router, moe_w_gate, moe_w_up, moe_w_down, ple_w_proj, ple_w_gate,
                 rope_cos, rope_sin, y_prompt, y_sample):
    with ExitStack() as ctx:
        def sb(name, shape, dt=F32):
            return ctx.enter_context(nc.sbuf_tensor(name, shape, dt))

        def sem(name):
            return ctx.enter_context(nc.semaphore(name))

        with nc.sbuf_tensor("ring", [P, NSLOT, SLOTW], F32) as ring, nc.sbuf_tensor("misc", [P, 6144], F32) as misc:
            pass
        sb("slots_0_to_3", [P, 4, SLOTW])
        wsplit = sb("wsplit", [P, NSPL, 2, KD, QW], F32R)
        sb("slot_7", [P, 1, SLOTW])
        xsplit = sb("xsplit", [P, KD, GRP, 2, NTOK], F32R)
        hsplit = sb("hsplit", [P, 2, KD, 2, NTOK], F32R)
        h = sb("h", [P, NJ, D])
        xn = sb("xn", [P, NJ, D])
        xt = sb("xt", [P, KD, T])
        work = sb("work", [P, D])
        ident = sb("ident", [P, P])
        ones = sb("ones", [P, P])
        diag32 = sb("diag32", [32, 32])
        token = sb("token", [P, NT])
        gains = sb("gains", [P, 64])
        ss = sb("ss", [P, 32])
        rs = sb("rs", [P, 32])
        eps = sb("eps", [P, 1])
        q_eps = sb("q_eps", [P, 1])
        cs = sb("cs", [P, 2, NT, ROPE // 2])
        wr = sb("wr", [P, 2, KD, NE])
        tri = sb("tri", [P, 4, P])
        fold = sb("fold", [P, NTOK])
        misc_moe = sb("sg_hid", [P, 2, HALF])
        blocks = sb("blocks", [P, 2 * LEVELS, P], mybir.dt.uint8)
        conv_w = sb("conv_w", [P, CONV * 24])
        wba = sb("wba", [P, KD, 32])
        ba = sb("ba", [P, NJ, 32])
        fac = sb("fac", [P, 8, NJ, 16])
        alog = sb("alog", [P, 2, 16])
        psum = ctx.enter_context(nc.psum_tensor("banks", [P, NBANK, HALF], F32))

        def slot(n, k, w):
            return ring[:, n, 0:k * w].rearrange("p (k w) -> p k w", k=k)

        lat = misc[:, 0:NJ * LAT].rearrange("p (j w) -> p j w", j=NJ)
        kvt = misc[:, 1792:1792 + T]
        krt = misc[:, 2304:2304 + T]
        prob = misc[:, 2816:3840].rearrange("p (b w) -> p b w", b=2)
        pt = misc[:, 3840:4864].rearrange("p (b w) -> p b w", b=2)
        krd = misc[:, 4864:5376].rearrange("p (j w) -> p j w", j=NJ)
        rt1 = misc[:, 5376:5504].rearrange("p (j w) -> p j w", j=NJ)
        rt2 = misc[:, 5504:5632].rearrange("p (j w) -> p j w", j=NJ)
        w_lat, w_qb, w_kvb = slot(0, KD, LAT), slot(1, 2, 1536), ring[:, 2, 0:2048]
        w_mo = [slot(3, HEADS, HALF), slot(4, HEADS, HALF)]
        qlt = ring[:, 1, 3072:4096].rearrange("p (k t) -> p k t", k=2)
        qrt = ring[:, 2, 2048:4096].rearrange("p (k t) -> p k t", k=4)
        qt, kt, vv = slot(5, HEADS, T), slot(6, HEADS, T), slot(7, NJ, D)
        qrn = xt[:, 0:4, :].rearrange("p k t -> p (k t)").rearrange("p (j w) -> p j w", j=NJ)
        qrr = xt[:, 4:8, :].rearrange("p k t -> p (k t)").rearrange("p (j w) -> p j w", j=NJ)
        ot = xn[:, :, :].rearrange("p j d -> p (j d)").rearrange("p (h t) -> p h t", h=HEADS)

        rows = misc[0:64, 5632:5760]

        oh = xt[:, 0:4, :]
        sc = xt[:, 4:8, :].rearrange("p q (j t) -> p q j t", j=NJ)
        ybuf = ring[:, 7, 0:2048].rearrange("p (s d) -> p s d", s=NS)
        pre = ring[:, 7, 2048:4096].rearrange("p (u c) -> p u c", u=4)
        sg, hid = (misc_moe[:, a, :].rearrange("p (k c) -> p k c", k=KD) for a in range(2))
        turned = [psum[:, 6 + a, :].rearrange("p (k c) -> p k c", k=KD) for a in range(2)]
        scs = work[:, 512:1024].rearrange("p (j t) -> p j t", j=NJ)
        aff = work[:, 0:64].rearrange("p (n s e) -> p n s e", n=NT, s=NS)
        afft = work[0:32, 64:320]
        topv = sb("topv", [32, CAP])
        topi = sb("topi", [32, CAP], U32)
        topf = sb("topf", [32, CAP])
        gcol = sb("gcol", [P, NQ, NS])
        spread = ring[0:32, 7, 0:1024].rearrange("p (a c) -> p a c", c=CAP)

        pin = misc[:, 0:1024].rearrange("p (j w) -> p j w", j=NJ)
        ptt = misc[:, 1024:2048].rearrange("p (k t) -> p k t", k=2)
        gate = misc[:, 2048:3072].rearrange("p (b w) -> p b w", b=2)
        prod = misc[:, 3072:4096].rearrange("p (b w) -> p b w", b=2)

        qkv = ring[:, 0:3, :].rearrange("p a w -> p (a w)").rearrange("p (c t) -> p c t", c=24)
        knat, vnat, znat = (slot(a, NJ, D).rearrange("p j (h w) -> p j h w", h=GH) for a in (3, 4, 5))
        pad = misc[:, 0:1040].rearrange("p (b s w) -> p b s w", b=2, s=NS)
        cacc = misc[:, 1040:2064].rearrange("p (b s w) -> p b s w", b=2, s=NS)
        sqb = misc[:, 2064:3088].rearrange("p (b w) -> p b w", b=2)
        rtb = misc[:, 3088:4112].rearrange("p (b w) -> p b w", b=2)
        conv_rows = misc[0:CONV * 24, 4112:4240]

        b_n_sq = misc[:, 0:1024].rearrange("p (h w) -> p h w", h=GH)

        def lanes(buf):
            return [buf(s).rearrange("p (h w) -> p h w", h=4) for s in range(NS)]

        b_gm, b_et, b_at, b_lt, b_n, b_u, b_t, b_z = (
            lanes(lambda s: ring[:, 6 + s, a * HALF:(a + 1) * HALF]) for a in range(8))
        b_r, b_kg, b_vn, b_s, b_tmp = (
            lanes(lambda s: misc[:, (5 * s + a) * HALF:(5 * s + a + 1) * HALF]) for a in range(5))
        o_acc = xn[:, :, :].rearrange("p j (h w) -> p j h w", h=GH)
        gw_out = [slot(2, KD, HALF), xt[:, :, :]]
        got = misc[:, 0:4096].rearrange("p (h t) -> p h t", h=HEADS)
        fg = misc[:, 5120:6144]

        banks = Ring()
        AV = ["act", "dve"]

        def stage(name, n, readers, add=True, before=None):
            st = Stage(sem, name, n, readers, before)
            if add:
                for i in range(n):
                    banks.add(st, i)
            return st

        s_vec = stage("gains", 2, ["dve"])
        s_xt0 = stage("xt", KD, AV)
        s_lat = stage("lat", NJ, AV)
        s_lt = stage("turned", 4, ["dve"])
        s_qn = stage("heads", HEADS, AV)
        s_qr = stage("q_rope", NJ, ["act"])
        s_kn = stage("k_nope", HEADS, AV, before=s_qn)
        s_v = stage("values", 2 * NJ, AV, before=s_kn)
        s_qrt = stage("q_rope_t", 4, ["dve"], before=s_lt)
        s_sc = stage("scores", 16, ["act"], add=False)
        s_pt = stage("prob_t", 16, ["dve"], add=False)
        s_ot = stage("attn_out", 16, ["act"], add=False)
        for i in range(16 + 2):
            if i < 16:
                banks.add(s_sc, i)
            if 1 <= i < 17:
                banks.add(s_pt, i - 1)
            if i >= 2:
                banks.add(s_ot, i - 2)
        s_mo = stage("mixer_proj", 2 * NJ, ["dve"])

        rounds = [(d, f, m) for d in range(2) for f in range(2) for m in range(2)]

        def gidx(r, s):
            return 2 * r + s

        def core_order():
            for r, (d, f, m) in enumerate(rounds):
                for name in ("decay", "kk", "qk", "lt", "n0"):
                    for s in range(NS):
                        yield name, gidx(r, s)
                for v in range(1, LEVELS):
                    for s in range(NS):
                        yield "z", 12 * r + 2 * (v - 1) + s
                    for s in range(NS):
                        if v < LEVELS - 1:
                            yield "dt", 10 * r + 2 * (v - 1) + s
                        yield "du", 12 * r + 2 * (v - 1) + s
                names = ("vn", "av", "st") if m == 0 else ("ks", "vn", "qs", "av")
                for name in names:
                    for s in range(NS):
                        yield name, (2 * (r // 2) + s if name in ("ks", "qs", "st") else gidx(r, s))

        class Layer:
            pass

        units = []
        for i in range(GRP):
            units += [("gate", i, 0), ("up", i, 0), ("gate", i, 1), ("up", i, 1)]
            if i:
                units += [("down", i - 1, 0), ("down", i - 1, 1)]
        units += [("down", GRP - 1, 0), ("down", GRP - 1, 1)]
        NU = len(units)
        unit_of = {u: n for n, u in enumerate(units)}
        NH = 2 * NU
        owner = ["pool" if m % 2 and (units[m // 2][0], units[m // 2][2]) in POOL_HALVES else "dve" for m in range(NH)]
        NH_DVE = owner.count("dve")

        def lo_count(m):
            return owner[:m + 1].count(owner[m])

        def unit_done(L, q, n):
            return q * NH + 2 * n + 2 + NSPL + L.done["w_used"]

        def lo_sem(m):
            return moe_sem["w_lo_" + owner[m]]

        def lo_value(L, q, m):
            return q * owner.count(owner[m]) + lo_count(m) + L.done["w_lo_" + owner[m]]

        PER_LAYER = {"gather_in_psum": 4 * NQ, "gather_hi": 16 * NQ, "gather_lo": 16 * NQ,
                     "w_hi": NH * NQ, "w_lo_dve": NH_DVE * NQ, "w_lo_pool": (NH - NH_DVE) * NQ, "w_used": NH * NQ,
                     "pre_read": 4 * NE, "folded": 2 * NE, "silu_done": NE, "hid_done": NE, "hid_hi": NE, "hid_lo": NE,
                     "y_hi": 4 * NE, "y_lo": 4 * NE,
                     "scat_in_psum": 8 * NQ, "scat_free": 8 * NQ, "sc_staged": NQ}
        moe_sem = {n: sem(n) for n in PER_LAYER}

        lay = []
        for l in range(2):
            L = Layer()
            lay.append(L)
            L.no = l
            L.rot = 3 * l
            prev = lay[0] if l else None
            if l == 1:
                s_xt1 = stage("xt", KD, AV, before=prev.s_pxt)
                s_qkv = stage("gdn_qkv", 24, ["act"])
                s_z = stage("gdn_z", 8, ["act"], before=s_qkv)
                s_ba = stage("gdn_ba", 1, ["dve"])
                s_cum = stage("decay_sums", 1, ["act"])
                s_nrm = stage("qk_norm", 16, ["act"])
                s_kt = stage("k_natural", GH, ["act"])
                s_vt = stage("v_natural", GH, ["dve"], before=s_qrt)
                core = {}
                for name, per, reader in (("decay", 1, "act"), ("kk", 1, "dve"), ("qk", 1, "dve"), ("lt", 1, "dve"),
                                          ("n0", 1, "dve"), ("z", 6, "act"), ("dt", 5, "dve"), ("du", 6, "dve"),
                                          ("ks", 1, "dve"), ("vn", 1, "act"), ("av", 1, "dve"), ("qs", 1, "dve"),
                                          ("st", 1, "act")):
                    few = name in ("ks", "qs", "st")
                    core[name] = stage("core_" + name, 16 * per // (2 if few else 1), [reader], add=False)
                for name, i in core_order():
                    banks.add(core[name], i)
                s_av = core["av"]
                s_gt = stage("gdn_out_t", KD, AV, before=s_v)
                s_go = stage("gdn_proj", 2 * NJ, ["dve"], before=s_mo)
            L.s_xt = stage("ffn_xt", KD, AV, before=s_xt1 if l else s_xt0)
            L.s_lg = stage("router", NJ, ["dve"], before=prev and prev.s_ib)
            L.s_at = stage("aff_t", 1, ["dve"], before=L.s_lg)
            L.s_gt = stage("top_t", 1, ["dve"], before=L.s_at)
            L.s_ib = stage("idx_rows", 2, ["dve"], before=L.s_gt)
            L.s_st = stage("scatter_t", 4, AV, before=prev and prev.s_st)
            L.done = {n: l * c for n, c in PER_LAYER.items()}
            L.s_pxt = stage("ple_xt", KD, AV, before=L.s_xt)
            L.s_ppt = stage("p_t", 2, ["dve"], before=prev and prev.s_ppt)
            L.s_pg = stage("ple_gate", 8, ["act"], add=False, before=prev and prev.s_pg)
            L.s_pp = stage("ple_proj", 8, ["dve"], add=False, before=prev and prev.s_pp)
            for i in range(8):
                banks.add(L.s_pg, i)
                banks.add(L.s_pp, i)

        vec_in, x_in, h_done, out_done = sem("vec_in"), sem("x_in"), sem("h_done"), sem("out_done")
        consts = sem("consts")
        act_link, dve_link, pool_link = sem("act_link"), sem("dve_link"), sem("pool_link")
        sq_done, sqrt_done, xn_done = sem("sq_done"), sem("sqrt_done"), sem("xn_done")
        loaded = [sem(f"slot{n}_loaded") for n in range(NSLOT)]
        loaded_b = [sem(f"slot{n}_second_half_loaded") for n in range(NRAW)]
        p_in = sem("p_in")
        soft_max_done, prob_done, prob_scaled = sem("row_max_done"), sem("prob_done"), sem("prob_scaled")
        lat_norm, rope_k, rope_q = sem("lat_norm"), sem("rope_k"), sem("rope_q")
        soft_e, soft_n = sem("router_exp"), sem("router_softmax")
        top_done, spread_done, onehot_done, gcol_done = sem("top_done"), sem("spread_done"), sem("onehot_done"), sem("gcol_done")
        gdn_in, alog_in = sem("w_ba_in"), sem("alog_in")
        conv_done, silu_q, sq16, rt_done, qk_done = (sem(x) for x in ("conv_done", "qkv_silu", "qk_squares", "qk_sqrt", "qk_scaled"))
        ba_exp, ba_dve, fac_done, masks = sem("ba_exp"), sem("ba_dve"), sem("factors"), sem("masks")
        gm_done, etm_done, ut_init, bv_done, kg_done, t0_done, r_done, o_done = (
            sem(x) for x in ("gm_done", "masked_decay", "ut_init", "bv_done", "kg_done", "t0_done", "rhs_done", "o_done"))
        o_norm, o_sqrt, gated = sem("o_norm"), sem("o_sqrt"), sem("gated")
        gdn_out1_in = sem("gdn_out1_in")
        fg_in = sem("fg_in")

        out_ready = sem("out_ready")

        block = ctx.enter_context(nc.Block())

        use = {}
        count = [0] * NSLOT

        def take(key, n):
            count[n] += 1
            use[key] = (loaded[n], 16 * count[n])

        for n, key in enumerate(["w_lat", "w_qb", "w_kvb", "w_mo0", "w_mo1"]):
            take(key, n)
        for l in range(2):
            lay[l].base = list(count)
            for n in range(NRAW):
                count[n] += 6 * NE // NRAW
            for n, key in enumerate([f"ple_g0{l}", f"ple_g1{l}", f"ple_p{l}"]):
                take(key, (lay[l].rot + n) % NRAW)
            if l == 0:
                for u in range(8):
                    take(f"gdn_in{u}", 6 + u % 2)
                take("gdn_out0", 2)

        expert_w = {"gate": moe_w_gate, "up": moe_w_up, "down": moe_w_down}

        def wait_use(eng, key):
            s, c = use[key]
            eng.wait_ge(s, c)

        norms = ["mix0", "ffn0", "ple0", "mix1", "ffn1", "ple1", "last"]
        norm_no = {n: i for i, n in enumerate(norms)}

        @block.sync
        def _(sp):
            for s, x in enumerate((x_prompt, x_sample)):
                sp.dma_start(h[:, NT * s:NT * s + NT, :],
                             x[0].rearrange("(j p) d -> p j d", p=P)).then_inc(x_in, 16)
            s0, _c = use["w_lat"]
            sp.dma_start(w_lat, mla_w_in[0].rearrange("(k p) n -> p k n", p=P)).then_inc(loaded[0], 16)
            sp.dma_start(w_qb, mla_w_qb[0].rearrange("(k p) n -> p k n", p=P)).then_inc(loaded[1], 16)
            sp.dma_start(w_kvb, mla_w_kvb[0]).then_inc(loaded[2], 16)
            wo = mla_w_out[0].rearrange("(k p) n -> p k n", p=P)
            for f in range(2):
                sp.dma_start(w_mo[f], wo[:, :, f * HALF:(f + 1) * HALF]).then_inc(loaded[3 + f], 16)

            def expert_half(l, q, m, slot_n):
                kind, i, f = units[m // 2]
                src = expert_w[kind][l].rearrange("e (k p) n -> e p k n", p=P)
                c = (m % 2) * QW
                to = loaded_b if m % 2 else loaded
                sp.dma_start(slot(slot_n, KD, HALF)[:, :, c:c + QW],
                             src[q * GRP + i, :, :, f * HALF + c:f * HALF + c + QW]).then_inc(to[slot_n], 16)

            def wait_half_used(L, q, m):
                sp.wait_ge(lo_sem(m), lo_value(L, q, m))

            for l in LAYERS:
                if l == 1:
                    sp.wait_ge(moe_sem["w_used"], unit_done(lay[0], NQ - 1, NU - 1))
                    sp.wait_ge(moe_sem["scat_in_psum"], 8 * NQ)
                    wi = gdn_w_in[0].rearrange("(k p) n -> p k n", p=P)
                    sp.dma_start(wba[:, :, :], wi[:, :, 4 * D:4 * D + 32]).then_inc(gdn_in, 16)
                    for u in range(8):
                        if u >= 2:
                            v = u - 2
                            sp.wait_ge(*(s_qkv.full(4 * v + 4) if v < 6 else s_z.full(4 * (v - 5))))
                        sp.dma_start(slot(6 + u % 2, KD, HALF), wi[:, :, u * HALF:(u + 1) * HALF]).then_inc(loaded[6 + u % 2], 16)
                    wo = gdn_w_out[0].rearrange("(k p) n -> p k n", p=P)
                    sp.wait_ge(*s_ba.full(1))
                    sp.dma_start(gw_out[1], wo[:, :, HALF:D]).then_inc(gdn_out1_in, 16)
                    sp.wait_ge(*s_vt.full(GH))
                    sp.dma_start(gw_out[0], wo[:, :, 0:HALF]).then_inc(loaded[2], 16)
                L = lay[l]
                if l == 0:
                    frees = [s_lat.full(NJ), s_qr.full(NJ), s_sc.full(16), s_mo.full(8)]
                else:
                    frees = [s_av.freed(15)] * NRAW
                    frees[2] = s_go.full(8)
                for n in range(NRAW):
                    sp.wait_ge(*frees[(n + L.rot) % NRAW])
                    for m in (2 * n, 2 * n + 1):
                        expert_half(l, 0, m, (n + L.rot) % NRAW)
                with sp.Fori(0, NQ - 1) as q:
                    for m in range(NH):
                        wait_half_used(L, q, m)
                        t = m + 2 * NRAW
                        expert_half(l, q + t // NH, t % NH, (t // 2 + L.rot) % NRAW)
                for m in range(2 * NRAW, NH):
                    wait_half_used(L, NQ - 1, m - 2 * NRAW)
                    expert_half(l, NQ - 1, m, (m // 2 + L.rot) % NRAW)
                wg = ple_w_gate[l].rearrange("(k p) n -> p k n", p=P)
                for f in range(2):
                    for m in range(2):
                        wait_half_used(L, NQ - 1, 2 * (NU - NRAW + f) + m)
                    n = (L.rot + f) % NRAW
                    sp.dma_start(slot(n, KD, HALF), wg[:, :, f * HALF:(f + 1) * HALF]).then_inc(loaded[n], 16)
                for m in range(2):
                    wait_half_used(L, NQ - 1, 2 * (NU - NRAW + 2) + m)
                n = (L.rot + 2) % NRAW
                sp.dma_start(slot(n, 2, D), ple_w_proj[l].rearrange("(k p) n -> p k n", p=P)).then_inc(loaded[n], 16)
                sp.wait_ge(moe_sem["w_used"], unit_done(L, NQ - 1, NU - 1))
                for s, x in enumerate((p_prompt, p_sample)):
                    sp.dma_start(pin[:, NT * s:NT * s + NT, :],
                                 x[l, 0].rearrange("(j p) d -> p j d", p=P)).then_inc(p_in, 16)
                if l == 1:
                    sp.dma_start(fg, final_norm_g.partition_broadcast(P)).then_inc(fg_in, 16)
            sp.wait_ge(out_ready, 4)
            for s, y in enumerate((y_prompt, y_sample)):
                sp.dma_start(y[0].rearrange("(j p) d -> p j d", p=P),
                             xn[:, NT * s:NT * s + NT, :]).then_inc(out_done, 16)
            sp.wait_ge(out_done, 32)


        def raw_half(L, m):
            return slot((m // 2 + L.rot) % NRAW, KD, HALF)[:, :, (m % 2) * QW:(m % 2 + 1) * QW]

        def split_lo(eng, L, q, m):
            eng.wait_ge(moe_sem["w_hi"], q * NH + m + 1 + L.done["w_hi"])
            b = m % NSPL
            eng.tensor_tensor(wsplit[:, b, 1, :, :], raw_half(L, m), wsplit[:, b, 0, :, :].bitcast(F32),
                              ALU.subtract).then_inc(lo_sem(m), 1)

        @block.gpsimd
        def _(pool):
            n = [0]

            def link(ins):
                n[0] += 1
                ins.then_inc(pool_link, 1)
                pool.wait_ge(pool_link, n[0])

            pool.dma_start(rows[ROW_MIX:ROW_MIX + 16, :], norm_mix_g.rearrange("l (k p) -> (l k) p", p=P)).then_inc(vec_in, 16)
            pool.dma_start(rows[ROW_FFN:ROW_FFN + 16, :], norm_ffn_g.rearrange("l (k p) -> (l k) p", p=P)).then_inc(vec_in, 16)
            pool.dma_start(rows[ROW_PLE:ROW_PLE + 16, :], norm_ple_g.rearrange("l (k p) -> (l k) p", p=P)).then_inc(vec_in, 16)
            pool.dma_start(rows[ROW_QN:ROW_QN + 2, :], mla_q_norm_g.rearrange("l (k p) -> (l k) p", p=P)).then_inc(vec_in, 16)
            pool.dma_start(rows[ROW_KVN:ROW_KVN + 1, :], mla_kv_norm_g).then_inc(vec_in, 16)
            pool.dma_start(cs[:, 0, :, :], rope_cos.rearrange("(j p) d -> p j d", p=P)).then_inc(vec_in, 16)
            pool.dma_start(cs[:, 1, :, :], rope_sin.rearrange("(j p) d -> p j d", p=P)).then_inc(vec_in, 16)
            for l in range(2):
                pool.dma_start(wr[:, l, :, :], moe_w_router[l].rearrange("(k p) n -> p k n", p=P)).then_inc(vec_in, 16)
            pool.dma_start(rows[ROW_GDN:ROW_GDN + 1, :], gdn_norm_g).then_inc(vec_in, 16)
            pool.dma_start(conv_rows, gdn_conv_w[0].rearrange("t (c p) -> (t c) p", p=P)).then_inc(vec_in, 16)
            pool.dma_start(alog[:, 0, :], gdn_A_log.rearrange("l d h -> (l d h)").partition_broadcast(P)).then_inc(alog_in, 16)
            pool.dma_start(alog[:, 1, :], gdn_dt_bias.rearrange("l d h -> (l d h)").partition_broadcast(P)).then_inc(alog_in, 16)
            link(pool.memset(ident[:, :], 0.0))
            link(pool.affine_select(out=ident[:, :], in_=ident[:, :], compare_op=ALU.not_equal, fill=1.0,
                                    base=0, pattern=[[-1, P]], channel_multiplier=1))
            link(pool.memset(fold[:, :], 0.0))
            for half in range(2):
                link(pool.affine_select(out=fold[:, :], in_=fold[:, :], compare_op=ALU.not_equal, fill=1.0,
                                        base=-NTOK * half, pattern=[[-1, NTOK]], channel_multiplier=1))
            link(pool.memset(diag32[:, :], 0.0))
            link(pool.affine_select(out=diag32[:, :], in_=diag32[:, :], compare_op=ALU.not_equal, fill=1.0,
                                    base=0, pattern=[[-1, 32]], channel_multiplier=1))
            link(pool.memset(ones[:, :], 1.0))
            link(pool.memset(eps[:, :], EPS))
            link(pool.memset(q_eps[:, :], EPS * P))
            link(pool.iota(token[:, :], pattern=[[P, NT]], base=0, channel_multiplier=1,
                           allow_small_or_imprecise_dtypes=True))
            link(pool.memset(tri[:, :, :], 1.0))
            for a, (cm, st, op) in enumerate(((-1, 1, ALU.is_ge), (1, -1, ALU.is_ge), (1, -1, ALU.is_gt), (-1, 1, ALU.is_gt))):
                link(pool.affine_select(out=tri[:, a, :], in_=tri[:, a, :], compare_op=op, fill=0.0, base=0,
                                        pattern=[[st, P]], channel_multiplier=cm))
            link(pool.iota(work[:, 0:P].bitcast(mybir.dt.int32), pattern=[[0, P]], base=0, channel_multiplier=1))
            link(pool.iota(work[:, P:2 * P].bitcast(mybir.dt.int32), pattern=[[1, P]], base=0, channel_multiplier=0))
            pool.sem_inc(consts, 1)
            def gdn_pool():
                pool.wait_ge(fac_done, 1)
                s_kt.wait_read(pool, GH - 1)
                s_vt.wait_read(pool, GH - 1)
                s_z.wait_read(pool, 7)
                for r, (d, f, m) in enumerate(rounds):
                    n = m if d == 0 else 1 - m
                    hs = slice(4 * f, 4 * f + 4)

                    def per_head(row, s):
                        return fac[:, row, NT * s + n, 8 * d + 4 * f:8 * d + 4 * f + 4].unsqueeze(2).to_broadcast([P, 4, P])

                    for s in range(NS):
                        if r:
                            pool.wait_ge(*core["decay"].full(gidx(r - 1, s) + 1))
                        pool.tensor_tensor(b_gm[s], tri[:, TRI_GT if d == 0 else TRI_LT, :].unsqueeze(1).to_broadcast([P, 4, P]),
                                           per_head(F_G, s), ALU.mult).then_inc(gm_done, 1)
                    for s in range(NS):
                        core["decay"].wait_read(pool, gidx(r, s))
                        if r:
                            pool.wait_ge(*core["av"].full(gidx(r - 1, s) + 1))
                        pool.tensor_tensor(b_at[s], tri[:, TRI_LE if d == 0 else TRI_GE, :].unsqueeze(1).to_broadcast([P, 4, P]),
                                           b_et[s], ALU.mult).then_inc(etm_done, 1)
                    for s in range(NS):
                        if r:
                            pool.wait_ge(*core["vn"].full(gidx(r - 1, s) + 1))
                        for b in (b_u[s], b_t[s]):
                            pool.tensor_copy(b, ident[:, :].unsqueeze(1).to_broadcast([P, 4, P])).then_inc(ut_init, 1)
                    for s in range(NS):
                        j = NT * s + n
                        pool.tensor_tensor(b_r[s], vnat[:, j, hs, :], per_head(F_BETA, s), ALU.mult).then_inc(bv_done, 1)
                        if m == 0:
                            if r:
                                pool.wait_ge(*core["st"].full(2 * (r // 2) - 2 + s + 1))
                            pool.tensor_tensor(b_kg[s], knat[:, j, hs, :], per_head(F_KG, s), ALU.mult).then_inc(kg_done, 1)

            for l in LAYERS:
                if l == 1:
                    gdn_pool()
                L = lay[l]
                L.s_st.wait_read(pool, 3)

                def step(q, last_step):
                    pool.wait_ge(moe_sem["scat_free"], q * 8 + 4 + L.done["scat_free"])
                    pool.wait_ge(consts, 1)
                    pool.tensor_copy(scs, sc[:, q, :, :]).then_inc(moe_sem["sc_staged"], 1)
                    for m in range(NSPL, NH if last_step else NH + NSPL):
                        if owner[m % NH] == "pool":
                            split_lo(pool, L, q + m // NH, m % NH)

                for m in range(NSPL):
                    if owner[m] == "pool":
                        split_lo(pool, L, 0, m)
                with pool.Fori(0, NQ - 1) as q:
                    step(q, False)
                step(NQ - 1, True)

        def norm_act(act, name, src, tag):
            i = norm_no[name]
            if i == 0:
                act.wait_ge(x_in, 32)
                act.wait_ge(masks, 1)
            else:
                act.wait_ge(h_done, i)
            for j in range(NJ):
                act.activation(work[:, :], h[:, j, :], ACT.Square,
                               accum_out=ss[:, j:j + 1]).then_inc(sq_done, 1)
                act.wait_ge(sq_done, 4 * i + j + 1)
            act.activation(rs[:, 0:NJ], ss[:, 0:NJ], ACT.Sqrt, bias=eps[:, :], scale=1.0 / D).then_inc(sqrt_done, 1)

        def xt_out(eng, which, st, row):
            for k in range(KD):
                if st.reader(k) != which:
                    continue
                eng.wait_ge(*st.full(k + 1))
                src, dst, g = psum[:, banks.bank(st, k), :], xt[:, k, :], gains[:, row + k:row + k + 1]
                if which == "act":
                    ins = eng.activation(dst, src, ACT.Copy, scale=g)
                else:
                    ins = eng.tensor_scalar(dst, src, g, None, ALU.mult)
                ins.then_inc(st.freed(k)[0], 1)

        @block.scalar
        def _(act):
            n = [0]

            def link(ins):
                n[0] += 1
                ins.then_inc(act_link, 1)
                act.wait_ge(act_link, n[0])

            def copy_out(st, i, dst, cols=HALF):
                act.wait_ge(*st.full(i + 1))
                act.activation(dst, psum[:, banks.bank(st, i), 0:cols], ACT.Copy).then_inc(st.freed(i)[0], 1)

            norm_act(act, "mix0", None, 0)
            s_vec.wait_read(act, 0)
            xt_out(act, "act", s_xt0, ROW_MIX)
            for j in range(0, NJ, 2):
                copy_out(s_lat, j, lat[:, j, :], LAT)
            s_lat.wait_read(act, NJ - 1)
            for j in range(NJ):
                link(act.activation(work[:, 0:QL], lat[:, j, 0:QL], ACT.Square, accum_out=ss[:, 4 + j:5 + j]))
                link(act.activation(work[:, 0:KVL], lat[:, j, QL:QL + KVL], ACT.Square, accum_out=ss[:, 8 + j:9 + j]))
            act.activation(rs[:, 4:8], ss[:, 4:8], ACT.Sqrt, bias=eps[:, :], scale=1.0 / QL).then_inc(sqrt_done, 1)
            act.activation(rs[:, 8:12], ss[:, 8:12], ACT.Sqrt, bias=eps[:, :], scale=1.0 / KVL).then_inc(sqrt_done, 1)
            for i in range(0, HEADS, 2):
                copy_out(s_qn, i, qt[:, i, :])
            for j in range(NJ):
                copy_out(s_qr, j, qrn[:, j, :])
            for i in range(0, HEADS, 2):
                copy_out(s_kn, i, kt[:, i, :])
            for i in range(0, 2 * NJ, 2):
                copy_out(s_v, i, vv[:, i // 2, 0:HALF])
            for i in range(18):
                if i < 16:
                    act.wait_ge(soft_max_done, i + 1)
                    if i >= 2:
                        act.wait_ge(*s_pt.full(i - 1))
                    b = banks.bank(s_sc, i)
                    for qh in range(2):
                        ins = act.activation(prob[:, i % 2, qh * SEQ:(qh + 1) * SEQ],
                                             psum[:, b, qh * SEQ:(qh + 1) * SEQ], ACT.Exp,
                                             bias=rs[:, 16 + 2 * (i % 2) + qh:17 + 2 * (i % 2) + qh], scale=SCALE,
                                             accum_out=ss[:, 16 + 2 * (i % 2) + qh:17 + 2 * (i % 2) + qh])
                        ins.then_inc(prob_done, 1)
                        if qh == 1:
                            act.wait_ge(prob_done, 2 * i + 2)
                            act.sem_inc(s_sc.freed(i)[0], 1)
                if i >= 2:
                    g = i - 2
                    s, hd = g // HEADS, g % HEADS
                    copy_out(s_ot, g, ot[:, hd, s * SEQ:(s + 1) * SEQ], SEQ)
            def gdn_act():
                norm_act(act, "mix1", None, 0)
                act.wait_ge(sq_done, 4 * norm_no["mix1"] + 4)
                xt_out(act, "act", s_xt1, ROW_MIX + 8)
                for c in range(25):
                    if c < 24:
                        act.wait_ge(*s_qkv.full(c + 1))
                        if c == 0:
                            act.wait_ge(masks, 2)
                        if c >= 2:
                            act.wait_ge(conv_done, c - 1)
                        act.activation(pad[:, c % 2, :, 2:258],
                                       psum[:, banks.bank(s_qkv, c), :].rearrange("p (s w) -> p s w", s=NS), ACT.Copy).then_inc(s_qkv.freed(c)[0], 1)
                    if c:
                        act.wait_ge(conv_done, c)
                        act.activation(qkv[:, c - 1, :].rearrange("p (s w) -> p s w", s=NS), cacc[:, (c - 1) % 2, :, :],
                                       ACT.Silu).then_inc(silu_q, 1)
                for i in range(8):
                    f, j = i // 4, i % 4
                    act.wait_ge(*s_z.full(i + 1))
                    act.activation(znat[:, j, 4 * f:4 * f + 4, :], psum[:, banks.bank(s_z, i), :].rearrange("p (h w) -> p h w", h=4),
                                   ACT.Silu).then_inc(s_z.freed(i)[0], 1)
                act.wait_ge(ba_dve, 1)
                act.activation(fac[:, F_X, :, :], fac[:, F_X, :, :], ACT.Exp, scale=-1.0).then_inc(ba_exp, 1)
                act.activation(fac[:, F_BETA, :, :], ba[:, :, 0:16], ACT.Exp, scale=-1.0).then_inc(ba_exp, 1)
                act.activation(alog[:, 0, :], alog[:, 0, :], ACT.Exp).then_inc(ba_exp, 1)
                act.wait_ge(ba_dve, 2)
                act.activation(fac[:, F_X, :, :], fac[:, F_X, :, :], ACT.Ln).then_inc(ba_exp, 1)
                act.wait_ge(*s_cum.full(1))
                cum = psum[:, banks.bank(s_cum, 0), 0:128].rearrange("p (a d j h) -> p a d j h", a=2, d=2, j=NJ)
                for d in range(2):
                    dh = slice(8 * d, 8 * d + 8)
                    act.activation(fac[:, F_EG, :, dh], cum[:, 0, d, :, :], ACT.Exp).then_inc(ba_exp, 1)
                    act.activation(fac[:, F_KG, :, dh], cum[:, 1, d, :, :], ACT.Exp).then_inc(ba_exp, 1)
                act.wait_ge(ba_exp, 8)
                act.sem_inc(s_cum.freed(0)[0], 1)
                for c in range(17):
                    if c < 16:
                        if c >= 2:
                            act.wait_ge(*s_nrm.full(c - 1))
                        if c == 0:
                            act.wait_ge(silu_q, 24)
                        act.activation(sqb[:, c % 2, :], qkv[:, c, :], ACT.Square).then_inc(sq16, 1)
                    if c:
                        k = c - 1
                        act.wait_ge(*s_nrm.full(k + 1))
                        if k >= 2:
                            act.wait_ge(qk_done, k - 1)
                        e, sc_ = (q_eps[:, :], float(P)) if k < GH else (eps[:, :], 1.0)
                        act.activation(rtb[:, k % 2, :], psum[:, banks.bank(s_nrm, k), :], ACT.Sqrt, bias=e, scale=sc_).then_inc(s_nrm.freed(k)[0], 1)
                for i in range(GH):
                    act.wait_ge(*s_kt.full(i + 1))
                    act.activation(knat[:, :, i, :], psum[:, banks.bank(s_kt, i), :].rearrange("p (j w) -> p j w", j=NJ),
                                   ACT.Copy).then_inc(s_kt.freed(i)[0], 1)

                def out(name, i, dst, func=ACT.Copy):
                    st = core[name]
                    act.wait_ge(*st.full(i + 1))
                    act.activation(dst, psum[:, banks.bank(st, i), :].rearrange("p (h w) -> p h w", h=4), func).then_inc(st.freed(i)[0], 1)

                s_z.wait_read(act, 7)
                for r, (d, f, m) in enumerate(rounds):
                    for s in range(NS):
                        if r:
                            core["kk"].wait_read(act, gidx(r - 1, s))
                            act.wait_ge(etm_done, gidx(r - 1, s) + 1)
                        out("decay", gidx(r, s), b_et[s], ACT.Exp)
                    for v in range(1, LEVELS):
                        for s in range(NS):
                            out("z", 12 * r + 2 * (v - 1) + s, b_z[s])
                    for s in range(NS):
                        out("vn", gidx(r, s), b_vn[s])
                    if m == 0:
                        for s in range(NS):
                            out("st", 2 * (r // 2) + s, b_s[s])
                act.wait_ge(o_norm, 1)
                act.activation(fac[:, F_Y, :, 0:8], fac[:, F_Y, :, 0:8], ACT.Sqrt, bias=eps[:, :], scale=1.0 / P).then_inc(o_sqrt, 1)
                for k in range(0, KD, 2):
                    act.wait_ge(*s_gt.full(k + 1))
                    act.activation(got[:, k, :], psum[:, banks.bank(s_gt, k), :], ACT.Copy,
                                   scale=gains[:, ROW_GDN:ROW_GDN + 1]).then_inc(s_gt.freed(k)[0], 1)

            for l in LAYERS:
                if l == 1:
                    gdn_act()
                L = lay[l]
                norm_act(act, f"ffn{l}", None, 0)
                xt_out(act, "act", L.s_xt, ROW_FFN + 8 * l)
                for j in range(NJ):
                    act.wait_ge(soft_n, 8 * l + 2 * j + 1)
                    act.activation(aff[:, j % NT, j // NT, :], work[:, 512 + 16 * j:528 + 16 * j], ACT.Exp,
                                   accum_out=ss[:, 20 + j:21 + j]).then_inc(soft_e, 1)
                act.wait_ge(gcol_done, l + 1)
                for q in range(0, NQ, 2):
                    act.wait_ge(*L.s_st.full(q + 1))
                    for s in range(NS):
                        ins = act.activation(sc[:, q, 2 * s:2 * s + 2, :], psum[:, banks.bank(L.s_st, q), s * SEQ:(s + 1) * SEQ], ACT.Copy,
                                             scale=gcol[:, q, s:s + 1])
                    ins.then_inc(L.s_st.freed(q)[0], 1)
                def split_hi(q, m):
                    n = m // 2
                    r = (n + L.rot) % NRAW
                    before = 16 * (6 * NE // NRAW) * L.no if m % 2 else 16 * L.base[r]
                    act.wait_ge((loaded_b if m % 2 else loaded)[r], q * (16 * NU // NRAW) + before + 16 * (n // NRAW + 1))
                    act.wait_ge(moe_sem["w_used"], q * NH + m + 1 + L.done["w_used"])
                    act.activation(wsplit[:, m % NSPL, 0, :, :], raw_half(L, m), ACT.Copy).then_inc(moe_sem["w_hi"], 1)

                def gather_hi(q):
                    for kk in range(KD):
                        if kk % 2 == 0:
                            act.wait_ge(moe_sem["gather_in_psum"], q * 4 + (kk // 2 + 1) + L.done["gather_in_psum"])
                        src = psum[:, kk // 2, (kk % 2) * 256:(kk % 2 + 1) * 256].rearrange("p (s e c) -> p e s c", s=NS, e=GRP)
                        for s in range(NS):
                            act.activation(xsplit[:, kk, :, 0, s * CAP:(s + 1) * CAP], src[:, :, s, :], ACT.Copy,
                                           scale=gains[:, ROW_FFN + 8 * l + kk:ROW_FFN + 8 * l + kk + 1]).then_inc(moe_sem["gather_hi"], 1)

                def step(q, last_step):

                    def silu(i):
                        act.wait_ge(moe_sem["folded"], q * (2 * GRP) + 2 * i + 1 + L.done["folded"])
                        act.activation(sg, turned[0], ACT.Silu).then_inc(moe_sem["silu_done"], 1)

                    def hidden_hi(i):
                        act.wait_ge(moe_sem["hid_done"], q * GRP + i + 1 + L.done["hid_done"])
                        act.activation(hsplit[:, i % 2, :, 0, :], hid, ACT.Copy).then_inc(moe_sem["hid_hi"], 1)

                    def y_hi(i, f):
                        if i == 0 and f == 0:
                            act.wait_ge(moe_sem["scat_free"], q * 8 + 4 + L.done["scat_free"])
                        act.wait_ge(moe_sem["w_used"], unit_done(L, q, unit_of[("down", i, f)]))
                        for s in range(NS):
                            act.activation(ybuf[32 * i:32 * i + 32, s, f * HALF:(f + 1) * HALF],
                                           psum[32 * s:32 * s + 32, 4 + f, :], ACT.Copy).then_inc(moe_sem["y_hi"], 1)

                    for m in range(NSPL, NH + NSPL):
                        if m < NH or not last_step:
                            split_hi(q + m // NH, m % NH)
                        for i in range(GRP):
                            last = 2 * unit_of[("up", i, 1)] - (i == GRP - 1)
                            if m == last + 7:
                                silu(i)
                            if m == last + 8:
                                hidden_hi(i)
                            for f in range(2):
                                if m == 2 * unit_of[("down", i, f)] + 4:
                                    y_hi(i, f)
                    if not last_step:
                        gather_hi(q + 1)

                for m in range(NSPL):
                    split_hi(0, m)
                gather_hi(0)
                with act.Fori(0, NQ - 1) as q:
                    step(q, False)
                step(NQ - 1, True)
                norm_act(act, f"ple{l}", None, 0)
                xt_out(act, "act", L.s_pxt, ROW_PLE + 8 * l)
                for i in range(8):
                    act.wait_ge(*L.s_pg.full(i + 1))
                    if i >= 2:
                        act.wait_ge(*L.s_pp.freed(i - 2))
                    act.activation(gate[:, i % 2, :], psum[:, banks.bank(L.s_pg, i), :],
                                   ACT.Sigmoid).then_inc(L.s_pg.freed(i)[0], 1)
            norm_act(act, "last", None, 0)

        @block.tensor
        def _(pe):
            def turn_xn(st):
                for k in range(KD):
                    banks.claim(pe, st, k)
                    for j in range(NJ):
                        mm = pe.transpose(psum[:, banks.bank(st, k), j * P:(j + 1) * P],
                                          xn[:, j, k * P:(k + 1) * P], ident[:, :])
                    mm.then_inc(st.filled, 1)

            def product(st, i, lhs, rhs, n, cols, last=True):
                banks.claim(pe, st, i)
                for k in range(n):
                    mm = pe.matmul(psum[:, banks.bank(st, i), 0:cols], lhs(k), rhs(k), start=(k == 0), stop=(k == n - 1))
                mm.then_inc(st.filled, 1)

            pe.wait_ge(consts, 1)
            pe.wait_ge(vec_in, 16 * 11)
            pe.transpose(psum[:, banks.bank(s_vec, 0), 0:NROWS], rows[0:NROWS, :], ident[0:NROWS, 0:NROWS]).then_inc(s_vec.filled, 1)
            pe.transpose(psum[:, banks.bank(s_vec, 1), 0:CONV * 24], conv_rows, ident[0:CONV * 24, 0:CONV * 24]).then_inc(s_vec.filled, 1)
            pe.wait_ge(xn_done, NJ)
            turn_xn(s_xt0)
            s_xt0.wait_read(pe, KD - 1)
            wait_use(pe, "w_lat")
            for j in range(NJ):
                product(s_lat, j, lambda k: xt[:, k, j * P:(j + 1) * P], lambda k: w_lat[:, k, :], KD, LAT)
            pe.wait_ge(lat_norm, 1)
            pe.wait_ge(rope_k, 1)
            for g in range(4):
                banks.claim(pe, s_lt, g)
                for j in range(NJ):
                    src = lat[:, j, g * P:(g + 1) * P] if g < 3 else krd[:, j, :]
                    mm = pe.transpose(psum[:, banks.bank(s_lt, g), j * P:(j + 1) * P], src, ident[:, :])
                mm.then_inc(s_lt.filled, 1)
            s_lt.wait_read(pe, 3)
            wait_use(pe, "w_qb")
            wq = w_qb.rearrange("p k (h w) -> p k h w", h=HEADS)
            for i in range(HEADS):
                product(s_qn, i, lambda k: wq[:, k, i, 0:NOPE], lambda k: qlt[:, k, :], 2, T)
            for j in range(NJ):
                product(s_qr, j, lambda k: qlt[:, k, j * P:(j + 1) * P], lambda k: wq[:, k, :, NOPE:NOPE + ROPE], 2, 512)
            wait_use(pe, "w_kvb")
            wkv = w_kvb.rearrange("p (h w) -> p h w", h=HEADS)
            for i in range(HEADS):
                product(s_kn, i, lambda k: wkv[:, i, 0:NOPE], lambda k: kvt, 1, T)
            for i in range(2 * NJ):
                j, f = i // 2, i % 2
                product(s_v, i, lambda k: kvt[:, j * P:(j + 1) * P], lambda k: wkv[:, 4 * f:4 * f + 4, NOPE:NOPE + DV], 1, HALF)
            pe.wait_ge(rope_q, 1)
            for g in range(4):
                banks.claim(pe, s_qrt, g)
                for j in range(NJ):
                    mm = pe.transpose(psum[:, banks.bank(s_qrt, g), j * P:(j + 1) * P], qrr[:, j, g * P:(g + 1) * P], ident[:, :])
                mm.then_inc(s_qrt.filled, 1)
            s_qn.wait_read(pe, HEADS - 1)
            s_kn.wait_read(pe, HEADS - 1)
            s_v.wait_read(pe, 2 * NJ - 1)
            s_qrt.wait_read(pe, 3)
            for i in range(18):
                if i < 16:
                    s, hd = i // HEADS, i % HEADS
                    banks.claim(pe, s_sc, i)
                    b = banks.bank(s_sc, i)
                    r0 = ROPE * (hd % 2)
                    keys = slice(s * SEQ, (s + 1) * SEQ)
                    for qh in range(2):
                        q0 = s * SEQ + qh * P
                        out = psum[:, b, qh * SEQ:(qh + 1) * SEQ]
                        pe.matmul(out, qt[:, hd, q0:q0 + P], kt[:, hd, keys], start=True, stop=False)
                        mm = pe.matmul(out, qrt[r0:r0 + ROPE, hd // 2, q0:q0 + P], krt[r0:r0 + ROPE, keys], start=False, stop=True)
                    mm.then_inc(s_sc.filled, 1)
                if 1 <= i < 17:
                    g = i - 1
                    pe.wait_ge(prob_scaled, g + 1)
                    banks.claim(pe, s_pt, g)
                    for kk in range(2):
                        for qh in range(2):
                            mm = pe.transpose(psum[:, banks.bank(s_pt, g), kk * SEQ + qh * P:kk * SEQ + (qh + 1) * P],
                                              prob[:, g % 2, qh * SEQ + kk * P:qh * SEQ + (kk + 1) * P], ident[:, :])
                    mm.then_inc(s_pt.filled, 1)
                if i >= 2:
                    g = i - 2
                    s, hd = g // HEADS, g % HEADS
                    s_pt.wait_read(pe, g)
                    product(s_ot, g, lambda k: vv[:, NT * s + k, hd * DV:(hd + 1) * DV],
                            lambda k: pt[:, g % 2, k * SEQ:(k + 1) * SEQ], 2, SEQ)
            s_ot.wait_read(pe, 15)
            for i in range(2 * NJ):
                j, f = i // 2, i % 2
                if i < 2:
                    wait_use(pe, f"w_mo{i}")
                product(s_mo, i, lambda k: ot[:, k, j * P:(j + 1) * P], lambda k: w_mo[f][:, k, :], HEADS, HALF)

            def gdn_pe():
                pe.wait_ge(xn_done, NJ * (norm_no["mix1"] + 1))
                turn_xn(s_xt1)
                s_xt1.wait_read(pe, KD - 1)
                for c in range(24):
                    if c % 4 == 0:
                        wait_use(pe, f"gdn_in{c // 4}")
                    w = slot(6 + (c // 4) % 2, KD, HALF)
                    product(s_qkv, c, lambda k: w[:, k, (c % 4) * P:(c % 4 + 1) * P], lambda k: xt[:, k, :], KD, T)
                for i in range(8):
                    f, j = i // 4, i % 4
                    if j == 0:
                        wait_use(pe, f"gdn_in{6 + f}")
                    product(s_z, i, lambda k: xt[:, k, j * P:(j + 1) * P], lambda k: slot(6 + f, KD, HALF)[:, k, :], KD, HALF)
                pe.wait_ge(gdn_in, 16)
                banks.claim(pe, s_ba, 0)
                for j in range(NJ):
                    for k in range(KD):
                        mm = pe.matmul(psum[:, banks.bank(s_ba, 0), 32 * j:32 * j + 32], xt[:, k, j * P:(j + 1) * P], wba[:, k, :],
                                       start=(k == 0), stop=(k == KD - 1))
                mm.then_inc(s_ba.filled, 1)
                pe.wait_ge(ba_dve, 3)
                banks.claim(pe, s_cum, 0)
                for a, masks_ in enumerate(((TRI_LE, TRI_GE), (TRI_GT, TRI_LT))):
                    for d in range(2):
                        c0 = 32 * (2 * a + d)
                        mm = pe.matmul(psum[:, banks.bank(s_cum, 0), c0:c0 + 32], tri[:, masks_[d], :], fac[:, F_G, :, 8 * d:8 * d + 8],
                                       start=True, stop=True)
                mm.then_inc(s_cum.filled, 1)
                for c in range(16):
                    pe.wait_ge(sq16, c + 1)
                    product(s_nrm, c, lambda k: ones[:, :], lambda k: sqb[:, c % 2, :], 1, T)
                for st, c0 in ((s_kt, GH), (s_vt, 2 * GH)):
                    if st is s_kt:
                        pe.wait_ge(qk_done, 16)
                    for i in range(GH):
                        banks.claim(pe, st, i)
                        for j in range(NJ):
                            mm = pe.transpose(psum[:, banks.bank(st, i), j * P:(j + 1) * P], qkv[:, c0 + i, j * P:(j + 1) * P], ident[:, :])
                        mm.then_inc(st.filled, 1)

                def four(name, i, lhs, rhs, turn=False):
                    st = core[name]
                    banks.claim(pe, st, i)
                    for g in range(4):
                        o = psum[:, banks.bank(st, i), g * P:(g + 1) * P]
                        mm = pe.transpose(o, lhs(g), ident[:, :]) if turn else pe.matmul(o, lhs(g), rhs(g), start=True, stop=True)
                    mm.then_inc(st.filled, 1)

                for r, (d, f, m) in enumerate(rounds):
                    n = m if d == 0 else 1 - m
                    tok = [slice((NT * s + n) * P, (NT * s + n + 1) * P) for s in range(NS)]
                    for s in range(NS):
                        pe.wait_ge(gm_done, gidx(r, s) + 1)
                        four("decay", gidx(r, s), lambda g: b_gm[s][:, g, :], lambda g: tri[:, TRI_LE if d == 0 else TRI_GE, :])
                    for s in range(NS):
                        four("kk", gidx(r, s), lambda g: qkv[:, GH + 4 * f + g, tok[s]], lambda g: qkv[:, GH + 4 * f + g, tok[s]])
                    for s in range(NS):
                        four("qk", gidx(r, s), lambda g: qkv[:, GH + 4 * f + g, tok[s]], lambda g: qkv[:, 4 * f + g, tok[s]])
                    for s in range(NS):
                        core["kk"].wait_read(pe, gidx(r, s))
                        four("lt", gidx(r, s), lambda g: b_lt[s][:, g, :], None, True)
                    for s in range(NS):
                        core["lt"].wait_read(pe, gidx(r, s))
                        four("n0", gidx(r, s), lambda g: b_n[s][:, g, :], None, True)
                    for v in range(1, LEVELS):
                        for s in range(NS):
                            if v == 1:
                                core["n0"].wait_read(pe, gidx(r, s))
                            else:
                                core["du"].wait_read(pe, 12 * r + 2 * (v - 2) + s)
                            four("z", 12 * r + 2 * (v - 1) + s, lambda g: b_n[s][:, g, :], lambda g: b_u[s][:, g, :])
                        for s in range(NS):
                            if v == 1:
                                pe.wait_ge(t0_done, gidx(r, s) + 1)
                            else:
                                core["dt"].wait_read(pe, 10 * r + 2 * (v - 2) + s)
                            core["z"].wait_read(pe, 12 * r + 2 * (v - 1) + s)
                            if v < LEVELS - 1:
                                four("dt", 10 * r + 2 * (v - 1) + s, lambda g: b_z[s][:, g, :], lambda g: b_t[s][:, g, :])
                            four("du", 12 * r + 2 * (v - 1) + s, lambda g: b_t[s][:, g, :], lambda g: b_z[s][:, g, :])
                    if m == 1:
                        for s in range(NS):
                            core["st"].wait_read(pe, 2 * (r // 2) + s)
                            four("ks", 2 * (r // 2) + s, lambda g: qkv[:, GH + 4 * f + g, tok[s]], lambda g: b_s[s][:, g, :])
                    for s in range(NS):
                        core["du"].wait_read(pe, 12 * r + 10 + s)
                        if m == 0:
                            pe.wait_ge(bv_done, gidx(r, s) + 1)
                        else:
                            pe.wait_ge(r_done, 2 * (r // 2) + s + 1)
                        four("vn", gidx(r, s), lambda g: b_u[s][:, g, :], lambda g: b_r[s][:, g, :])
                    if m == 1:
                        for s in range(NS):
                            four("qs", 2 * (r // 2) + s, lambda g: qkv[:, 4 * f + g, tok[s]], lambda g: b_s[s][:, g, :])
                    for s in range(NS):
                        core["vn"].wait_read(pe, gidx(r, s))
                        core["qk"].wait_read(pe, gidx(r, s))
                        four("av", gidx(r, s), lambda g: b_at[s][:, g, :], lambda g: b_vn[s][:, g, :])
                    if m == 0:
                        for s in range(NS):
                            pe.wait_ge(kg_done, 2 * (r // 2) + s + 1)
                            four("st", 2 * (r // 2) + s, lambda g: b_kg[s][:, g, :], lambda g: b_vn[s][:, g, :])
                for k in range(KD):
                    pe.wait_ge(gated, NJ)
                    banks.claim(pe, s_gt, k)
                    for j in range(NJ):
                        mm = pe.transpose(psum[:, banks.bank(s_gt, k), j * P:(j + 1) * P], o_acc[:, j, k, :], ident[:, :])
                    mm.then_inc(s_gt.filled, 1)
                s_gt.wait_read(pe, KD - 1)
                wait_use(pe, "gdn_out0")
                pe.wait_ge(gdn_out1_in, 16)
                for i in range(2 * NJ):
                    j, f = i // 2, i % 2
                    product(s_go, i, lambda k: got[:, k, j * P:(j + 1) * P], lambda k: gw_out[f][:, k, :], KD, HALF)

            for l in LAYERS:
                if l == 1:
                    gdn_pe()
                L = lay[l]
                pe.wait_ge(xn_done, NJ * (norm_no[f"ffn{l}"] + 1))
                turn_xn(L.s_xt)
                L.s_xt.wait_read(pe, KD - 1)
                for j in range(NJ):
                    product(L.s_lg, j, lambda k: xt[:, k, j * P:(j + 1) * P], lambda k: wr[:, l, k, :], KD, NE)
                pe.wait_ge(soft_n, 8 * l + 8)
                banks.claim(pe, L.s_at, 0)
                for t in range(NT):
                    mm = pe.transpose(psum[0:32, banks.bank(L.s_at, 0), t * P:(t + 1) * P],
                                      aff[:, t, :, :].rearrange("p s e -> p (s e)"), ident[:, :])
                mm.then_inc(L.s_at.filled, 1)
                pe.wait_ge(top_done, l + 1)
                banks.claim(pe, L.s_gt, 0)
                pe.transpose(psum[0:32, banks.bank(L.s_gt, 0), 0:32], topv[:, :], ident[0:32, 0:32]).then_inc(L.s_gt.filled, 1)
                pe.wait_ge(spread_done, l + 1)
                for s in range(NS):
                    product(L.s_ib, s, lambda k: ones[0:32, :], lambda k: spread[:, 16 * s:16 * s + 16, :], 1, HALF)
                pe.wait_ge(onehot_done, 4 * (l + 1))
                for q in range(NQ):
                    banks.claim(pe, L.s_st, q)
                    for j in range(NJ):
                        mm = pe.transpose(psum[:, banks.bank(L.s_st, q), j * P:(j + 1) * P],
                                          oh[:, j, q * P:(q + 1) * P], ident[:, :])
                    mm.then_inc(L.s_st.filled, 1)
                L.s_st.wait_read(pe, 3)
                pe.wait_ge(gcol_done, l + 1)
                def gather(q):
                    for kp in range(4):
                        for k in range(2):
                            for s in range(NS):
                                o = psum[:, kp, k * 256 + s * P:k * 256 + (s + 1) * P]
                                c0 = (2 * kp + k) * P
                                for t in range(NT):
                                    mm = pe.matmul(o, xn[:, NT * s + t, c0:c0 + P], oh[:, NT * s + t, bass.ds(q * P, P)],
                                                   start=(t == 0), stop=(t == NT - 1))
                        mm.then_inc(moe_sem["gather_in_psum"], 1)

                def step(q, last_step):
                    pe.wait_ge(moe_sem["gather_lo"], (q + 1) * 16 + L.done["gather_lo"])

                    def unit_product(kind, i, f, bank, tokens):
                        for b in range(2):
                            m = 2 * unit_of[(kind, i, f)] + b
                            pe.wait_ge(lo_sem(m), lo_value(L, q, m))
                            for k in range(KD):
                                for part in range(2):
                                    mm = pe.matmul(psum[:, bank, b * QW:(b + 1) * QW], tokens(k).rearrange("p a c -> p (a c)"),
                                                   wsplit[:, m % NSPL, part, k, :],
                                                   start=(k == 0 and part == 0), stop=(k == KD - 1 and part == 1))
                            mm.then_inc(moe_sem["w_used"], 1)

                    def gate_up(i, u):
                        kind, f = ("gate", "up")[u % 2], u // 2
                        if i:
                            pe.wait_ge(moe_sem["pre_read"], q * (4 * GRP) + 4 * i - 4 + u + 1 + L.done["pre_read"])
                        unit_product(kind, i, f, u, lambda k: xsplit[:, k, i, :, :])

                    def fold_turn(i):
                        if i:
                            pe.wait_ge(moe_sem["hid_done"], q * GRP + i + L.done["hid_done"])
                        else:
                            pe.wait_ge(moe_sem["scat_free"], q * 8 + 4 + L.done["scat_free"])
                        pe.wait_ge(moe_sem["pre_read"], q * (4 * GRP) + 4 * i + 4 + L.done["pre_read"])
                        for a in range(2):
                            for ft in range(KD):
                                mm = pe.matmul(turned[a][:, ft, :], pre[:, 2 * (ft // 4) + a, (ft % 4) * P:(ft % 4 + 1) * P], fold[:, :],
                                               start=True, stop=True)
                            mm.then_inc(moe_sem["folded"], 1)

                    def down(i, f):
                        pe.wait_ge(moe_sem["hid_lo"], q * GRP + i + 1 + L.done["hid_lo"])
                        if i:
                            pe.wait_ge(moe_sem["y_lo"], q * 16 + 4 * (i - 1) + 2 * f + 2 + L.done["y_lo"])
                        unit_product("down", i, f, 4 + f, lambda k: hsplit[:, i % 2, k, :, :])

                    for u in range(4):
                        gate_up(0, u)
                    for i in range(1, GRP):
                        for u in range(4):
                            gate_up(i, u)
                            if i == 1 and u == 0:
                                fold_turn(0)
                        for f in range(2):
                            down(i - 1, f)
                            if f == 0:
                                fold_turn(i)
                    for f in range(2):
                        down(GRP - 1, f)
                    if not last_step:
                        gather(q + 1)
                    pe.wait_ge(moe_sem["sc_staged"], q + 1 + L.done["sc_staged"])
                    pe.wait_ge(moe_sem["y_lo"], (q + 1) * 16 + L.done["y_lo"])
                    for g in range(8):
                        j, f = g // 2, g % 2
                        if g >= 4:
                            pe.wait_ge(moe_sem["scat_free"], q * 8 + (g + 1) + L.done["scat_free"])
                        pe.matmul(psum[:, 4 + g % 4, :], scs[:, j, :], ybuf[:, j // NT, f * HALF:(f + 1) * HALF],
                                  start=True, stop=True).then_inc(moe_sem["scat_in_psum"], 1)

                gather(0)
                with pe.Fori(0, NQ - 1) as q:
                    step(q, False)
                step(NQ - 1, True)
                pe.wait_ge(xn_done, NJ * (norm_no[f"ple{l}"] + 1))
                turn_xn(L.s_pxt)
                pe.wait_ge(p_in, 32 * (l + 1))
                for k in range(2):
                    banks.claim(pe, L.s_ppt, k)
                    for j in range(NJ):
                        mm = pe.transpose(psum[:, banks.bank(L.s_ppt, k), j * P:(j + 1) * P], pin[:, j, k * P:(k + 1) * P], ident[:, :])
                    mm.then_inc(L.s_ppt.filled, 1)
                L.s_pxt.wait_read(pe, KD - 1)
                L.s_ppt.wait_read(pe, 1)
                for key in (f"ple_g0{l}", f"ple_g1{l}", f"ple_p{l}"):
                    wait_use(pe, key)
                wp = slot((L.rot + 2) % NRAW, 2, D)
                for i in range(8):
                    j, f = i // 2, i % 2
                    product(L.s_pg, i, lambda k: xt[:, k, j * P:(j + 1) * P], lambda k: slot((L.rot + f) % NRAW, KD, HALF)[:, k, :], KD, HALF)
                    product(L.s_pp, i, lambda k: ptt[:, k, j * P:(j + 1) * P], lambda k: wp[:, k, f * HALF:(f + 1) * HALF], 2, HALF)

        @block.vector
        def _(dve):
            n = [0]

            def link(ins):
                n[0] += 1
                ins.then_inc(dve_link, 1)
                dve.wait_ge(dve_link, n[0])

            def norm(name):
                i = norm_no[name]
                dve.wait_ge(sqrt_done, i + 1 + (2 if i else 0))
                link(dve.reciprocal(rs[:, 24:24 + NJ], rs[:, 0:NJ]))
                for j in range(NJ):
                    dve.tensor_scalar(xn[:, j, :], h[:, j, :], rs[:, 24 + j:25 + j], None, ALU.mult).then_inc(xn_done, 1)

            def copy_out(st, i, dst, cols=HALF):
                dve.wait_ge(*st.full(i + 1))
                dve.tensor_copy(dst, psum[:, banks.bank(st, i), 0:cols]).then_inc(st.freed(i)[0], 1)

            dve.wait_ge(*s_vec.full(1))
            dve.tensor_copy(gains[:, 0:NROWS], psum[:, banks.bank(s_vec, 0), 0:NROWS]).then_inc(s_vec.freed(0)[0], 1)
            dve.wait_ge(*s_vec.full(2))
            dve.tensor_copy(conv_w[:, :], psum[:, banks.bank(s_vec, 1), 0:CONV * 24]).then_inc(s_vec.freed(1)[0], 1)
            s_vec.wait_read(dve, 1)
            row, col, dif, sh = (work[:, a * P:(a + 1) * P].bitcast(mybir.dt.int32) for a in range(4))
            link(dve.tensor_tensor(dif, row, col, ALU.bitwise_xor))
            for v in range(LEVELS):
                link(dve.tensor_single_scalar(sh, dif, v, ALU.logical_shift_right))
                for side, m in enumerate((TRI_GT, TRI_LT)):
                    ins = dve.scalar_tensor_tensor(out=blocks[:, 2 * v + side, :], in0=sh, scalar=1.0, in1=tri[:, m, :],
                                                   op0=ALU.is_equal, op1=ALU.mult)
                    if side:
                        link(ins)
            dve.sem_inc(masks, 1)
            norm("mix0")
            xt_out(dve, "dve", s_xt0, ROW_MIX)
            for j in range(1, NJ, 2):
                copy_out(s_lat, j, lat[:, j, :], LAT)
            s_lat.wait_read(dve, NJ - 1)
            c4 = cs[:, 0, :, :]
            s4 = cs[:, 1, :, :]
            for s in range(NS):
                jj = slice(NT * s, NT * s + NT)
                x1, x2 = lat[:, jj, 384:416], lat[:, jj, 416:448]
                for d0 in (0, ROPE):
                    link(dve.tensor_tensor(rt1[:, jj, :], x1, c4, ALU.mult))
                    link(dve.tensor_tensor(rt2[:, jj, :], x2, s4, ALU.mult))
                    link(dve.tensor_tensor(krd[:, jj, d0:d0 + 32], rt1[:, jj, :], rt2[:, jj, :], ALU.subtract))
                    link(dve.tensor_tensor(rt1[:, jj, :], x2, c4, ALU.mult))
                    link(dve.tensor_tensor(rt2[:, jj, :], x1, s4, ALU.mult))
                    ins = dve.tensor_tensor(krd[:, jj, d0 + 32:d0 + 64], rt1[:, jj, :], rt2[:, jj, :], ALU.add)
                    if s == 1 and d0:
                        ins.then_inc(rope_k, 1)
                    else:
                        link(ins)
            dve.wait_ge(sqrt_done, 3)
            link(dve.reciprocal(rs[:, 4:12], rs[:, 4:12]))
            for j in range(NJ):
                link(dve.tensor_scalar(lat[:, j, 0:QL], lat[:, j, 0:QL], rs[:, 4 + j:5 + j], None, ALU.mult))
                ins = dve.tensor_scalar(lat[:, j, QL:QL + KVL], lat[:, j, QL:QL + KVL], rs[:, 8 + j:9 + j], None, ALU.mult)
                if j < NJ - 1:
                    link(ins)
                else:
                    ins.then_inc(lat_norm, 1)
            for g in range(4):
                dve.wait_ge(*s_lt.full(g + 1))
                dst = qlt[:, g, :] if g < 2 else (kvt if g == 2 else krt)
                src = psum[:, banks.bank(s_lt, g), :]
                if g < 3:
                    dve.tensor_scalar(dst, src, gains[:, ROW_QN + g:ROW_QN + g + 1], None, ALU.mult).then_inc(s_lt.freed(g)[0], 1)
                else:
                    dve.tensor_copy(dst, src).then_inc(s_lt.freed(g)[0], 1)
            for i in range(1, HEADS, 2):
                copy_out(s_qn, i, qt[:, i, :])
            for j in range(NJ):
                s_qr.wait_read(dve, j)
                v = qrn[:, j, :].rearrange("p (h w) -> p h w", h=HEADS)
                o = qrr[:, j, :].rearrange("p (h w) -> p h w", h=HEADS)
                cb = cs[:, 0, j % NT, :].unsqueeze(1).to_broadcast([P, HEADS, 32])
                sb_ = cs[:, 1, j % NT, :].unsqueeze(1).to_broadcast([P, HEADS, 32])
                w1 = work[:, 0:256].rearrange("p (h w) -> p h w", h=HEADS)
                w2 = work[:, 256:512].rearrange("p (h w) -> p h w", h=HEADS)
                w3 = work[:, 512:768].rearrange("p (h w) -> p h w", h=HEADS)
                w4 = work[:, 768:1024].rearrange("p (h w) -> p h w", h=HEADS)
                dve.tensor_tensor(w1, v[:, :, 0:32], cb, ALU.mult)
                dve.tensor_tensor(w2, v[:, :, 32:64], sb_, ALU.mult)
                dve.tensor_tensor(w3, v[:, :, 32:64], cb, ALU.mult)
                link(dve.tensor_tensor(w4, v[:, :, 0:32], sb_, ALU.mult))
                dve.tensor_tensor(o[:, :, 0:32], w1, w2, ALU.subtract)
                ins = dve.tensor_tensor(o[:, :, 32:64], w3, w4, ALU.add)
                if j < NJ - 1:
                    link(ins)
                else:
                    ins.then_inc(rope_q, 1)
            for i in range(1, HEADS, 2):
                copy_out(s_kn, i, kt[:, i, :])
            for i in range(1, 2 * NJ, 2):
                copy_out(s_v, i, vv[:, i // 2, HALF:D])
            for g in range(4):
                copy_out(s_qrt, g, qrt[:, g, :])
            for i in range(17):
                if i < 16:
                    b = i % 2
                    dve.wait_ge(*s_sc.full(i + 1))
                    if i >= 2:
                        dve.wait_ge(prob_done, 2 * i - 2)
                    link(dve.tensor_reduce(rs[:, 20 + 2 * b:22 + 2 * b],
                                           psum[:, banks.bank(s_sc, i), :].rearrange("p (a k) -> p a k", a=2),
                                           AX_X, ALU.max))
                    dve.tensor_scalar(rs[:, 16 + 2 * b:18 + 2 * b], rs[:, 20 + 2 * b:22 + 2 * b], -SCALE, None,
                                      ALU.mult).then_inc(soft_max_done, 1)
                if i >= 1:
                    g = i - 1
                    if g >= 1:
                        dve.wait_ge(*s_pt.full(g))
                        if g >= 3:
                            dve.wait_ge(*s_ot.full(g - 2))
                        dve.tensor_copy(pt[:, (g - 1) % 2, :], psum[:, banks.bank(s_pt, g - 1), :]).then_inc(s_pt.freed(g - 1)[0], 1)
                    b = g % 2
                    dve.wait_ge(prob_done, 2 * g + 2)
                    link(dve.reciprocal(ss[:, 24 + 2 * b:26 + 2 * b], ss[:, 16 + 2 * b:18 + 2 * b]))
                    for qh in range(2):
                        ins = dve.tensor_scalar(prob[:, b, qh * SEQ:(qh + 1) * SEQ], prob[:, b, qh * SEQ:(qh + 1) * SEQ],
                                                ss[:, 24 + 2 * b + qh:25 + 2 * b + qh], None, ALU.mult)
                        if qh:
                            ins.then_inc(prob_scaled, 1)
            copy_out(s_pt, 15, pt[:, 1, :])
            for i in range(2 * NJ):
                j, f = i // 2, i % 2
                dve.wait_ge(*s_mo.full(i + 1))
                hv = h[:, j, f * HALF:(f + 1) * HALF]
                dve.tensor_tensor(hv, hv, psum[:, banks.bank(s_mo, i), :], ALU.add).then_inc(s_mo.freed(i)[0], 1)
            s_mo.wait_read(dve, 2 * NJ - 1)
            dve.sem_inc(h_done, 1)

            def gdn_dve():
                norm("mix1")
                xt_out(dve, "dve", s_xt1, ROW_MIX + 8)
                link(dve.memset(pad[:, :, :, 0:2], 0.0))
                dve.memset(pad[:, :, :, 258:260], 0.0).then_inc(masks, 1)
                for c in range(24):
                    s_qkv.wait_read(dve, c)
                    if c >= 2:
                        dve.wait_ge(silu_q, c - 1)
                    a = cacc[:, c % 2, :, :]
                    for t in range(CONV):
                        x = pad[:, c % 2, :, t:t + SEQ]
                        w = conv_w[:, 24 * t + c:24 * t + c + 1]
                        if t == 0:
                            ins = dve.tensor_scalar(a, x, w, None, ALU.mult)
                        else:
                            ins = dve.scalar_tensor_tensor(out=a, in0=x, scalar=w, in1=a, op0=ALU.mult, op1=ALU.add)
                        if t < CONV - 1:
                            link(ins)
                        else:
                            ins.then_inc(conv_done, 1)
                dve.wait_ge(*s_ba.full(1))
                dve.tensor_copy(ba[:, :, :], psum[:, banks.bank(s_ba, 0), 0:128].rearrange("p (j w) -> p j w", j=NJ)).then_inc(s_ba.freed(0)[0], 1)
                s_ba.wait_read(dve, 0)
                dve.wait_ge(alog_in, 32)
                x, y = fac[:, F_X, :, :], fac[:, F_Y, :, :]
                link(dve.tensor_tensor(y, ba[:, :, 16:32], alog[:, 1, :].unsqueeze(1).to_broadcast([P, NJ, 16]), ALU.add))
                dve.scalar_tensor_tensor(out=x, in0=y, scalar=-1.0, in1=y, op0=ALU.mult, op1=ALU.max).then_inc(ba_dve, 1)

                def scale_qk():
                    for c in range(16):
                        s_nrm.wait_read(dve, c)
                        link(dve.reciprocal(rtb[:, c % 2, :], rtb[:, c % 2, :]))
                        dve.tensor_tensor(qkv[:, c, :], qkv[:, c, :], rtb[:, c % 2, :], ALU.mult).then_inc(qk_done, 1)

                dve.wait_ge(ba_exp, 3)
                b, nb = fac[:, F_BETA, :, :], fac[:, F_NBETA, :, :]
                link(dve.tensor_scalar(b, b, 1.0, None, ALU.add))
                link(dve.reciprocal(b, b))
                link(dve.tensor_scalar(nb, b, -1.0, None, ALU.mult))
                dve.tensor_scalar(x, x, 1.0, None, ALU.add).then_inc(ba_dve, 1)
                dve.wait_ge(ba_exp, 4)
                link(dve.scalar_tensor_tensor(out=x, in0=y, scalar=0.0, in1=x, op0=ALU.max, op1=ALU.add))
                link(dve.tensor_scalar(x, x, -1.0, None, ALU.mult))
                dve.tensor_tensor(fac[:, F_G, :, :], x, alog[:, 0, :].unsqueeze(1).to_broadcast([P, NJ, 16]), ALU.mult).then_inc(ba_dve, 1)
                dve.wait_ge(ba_exp, 8)
                dve.tensor_tensor(fac[:, F_BEG, :, :], fac[:, F_EG, :, :], b, ALU.mult).then_inc(fac_done, 1)
                scale_qk()
                for i in range(GH):
                    dve.wait_ge(*s_vt.full(i + 1))
                    dve.tensor_copy(vnat[:, :, i, :], psum[:, banks.bank(s_vt, i), :].rearrange("p (j w) -> p j w", j=NJ)).then_inc(s_vt.freed(i)[0], 1)

                def bank4(name, i):
                    dve.wait_ge(core[name].filled, i + 1)
                    return psum[:, banks.bank(core[name], i), :].rearrange("p (h w) -> p h w", h=4)

                def done(name, i, ins):
                    ins.then_inc(core[name].freed(i)[0], 1)

                for r, (d, f, m) in enumerate(rounds):
                    n = m if d == 0 else 1 - m
                    hs = slice(4 * f, 4 * f + 4)

                    def per_head(row, s):
                        return fac[:, row, NT * s + n, 8 * d + 4 * f:8 * d + 4 * f + 4].unsqueeze(2).to_broadcast([P, 4, P])

                    def block(v, turned):
                        side = (d + turned) % 2
                        return blocks[:, 2 * v + side, :].unsqueeze(1).to_broadcast([P, 4, P])

                    for s in range(NS):
                        i = gidx(r, s)
                        core["decay"].wait_read(dve, i)
                        done("kk", i, dve.tensor_tensor(b_lt[s], b_et[s], bank4("kk", i), ALU.mult))
                    for s in range(NS):
                        i = gidx(r, s)
                        dve.wait_ge(etm_done, i + 1)
                        done("qk", i, dve.tensor_tensor(b_at[s], b_at[s], bank4("qk", i), ALU.mult))
                    for s in range(NS):
                        i = gidx(r, s)
                        done("lt", i, dve.tensor_tensor(b_n[s], per_head(F_NBETA, s), bank4("lt", i), ALU.mult))
                    for s in range(NS):
                        i = gidx(r, s)
                        dve.wait_ge(ut_init, 4 * r + 2 * s + 2)
                        core["lt"].wait_read(dve, i)
                        done("n0", i, dve.copy_predicated(b_u[s], block(0, 1), bank4("n0", i)))
                        dve.copy_predicated(b_t[s], block(0, 0), b_n[s]).then_inc(t0_done, 1)
                    for v in range(1, LEVELS):
                        for s in range(NS):
                            i, k = 12 * r + 2 * (v - 1) + s, 10 * r + 2 * (v - 1) + s
                            du = bank4("du", i)
                            core["n0"].wait_read(dve, gidx(r, s)) if v == 1 else core["du"].wait_read(dve, i - 2)
                            done("du", i, dve.copy_predicated(b_u[s], block(v, 1), du))
                            if v < LEVELS - 1:
                                dve.wait_ge(t0_done, gidx(r, s) + 1) if v == 1 else core["dt"].wait_read(dve, k - 2)
                                done("dt", k, dve.copy_predicated(b_t[s], block(v, 0), bank4("dt", k)))
                    if m == 1:
                        for s in range(NS):
                            i = 2 * (r // 2) + s
                            dve.wait_ge(bv_done, gidx(r, s) + 1)
                            done("ks", i, dve.tensor_tensor(b_tmp[s], per_head(F_BEG, s), bank4("ks", i), ALU.mult))
                            core["ks"].wait_read(dve, i)
                            dve.tensor_tensor(b_r[s], b_r[s], b_tmp[s], ALU.subtract).then_inc(r_done, 1)
                        for s in range(NS):
                            i = 2 * (r // 2) + s
                            dve.wait_ge(r_done, i + 1)
                            done("qs", i, dve.tensor_tensor(b_tmp[s], per_head(F_EG, s), bank4("qs", i), ALU.mult))
                    for s in range(NS):
                        i = gidx(r, s)
                        o = o_acc[:, NT * s + n, hs, :]
                        if m == 1:
                            core["qs"].wait_read(dve, 2 * (r // 2) + s)
                            if d == 1:
                                link(dve.tensor_tensor(b_tmp[s], b_tmp[s], o, ALU.add))
                            done("av", i, dve.tensor_tensor(o, b_tmp[s], bank4("av", i), ALU.add))
                        elif d == 1:
                            done("av", i, dve.tensor_tensor(o, o, bank4("av", i), ALU.add))
                        else:
                            done("av", i, dve.tensor_copy(o, bank4("av", i)))
                core["av"].wait_read(dve, 15)
                for j in range(NJ):
                    link(dve.tensor_tensor(b_n_sq, o_acc[:, j, :, :], o_acc[:, j, :, :], ALU.mult))
                    ins = dve.tensor_reduce(fac[:, F_Y, j, 0:8], b_n_sq, AX_X, ALU.add)
                    if j < NJ - 1:
                        link(ins)
                    else:
                        ins.then_inc(o_norm, 1)
                dve.wait_ge(o_sqrt, 1)
                link(dve.reciprocal(fac[:, F_Y, :, 0:8], fac[:, F_Y, :, 0:8]))
                for j in range(NJ):
                    o = o_acc[:, j, :, :]
                    link(dve.tensor_tensor(o, o, fac[:, F_Y, j, 0:8].unsqueeze(2).to_broadcast([P, GH, P]), ALU.mult))
                    dve.tensor_tensor(o, o, znat[:, j, :, :], ALU.mult).then_inc(gated, 1)
                for k in range(1, KD, 2):
                    dve.wait_ge(*s_gt.full(k + 1))
                    dve.tensor_scalar(got[:, k, :], psum[:, banks.bank(s_gt, k), :], gains[:, ROW_GDN:ROW_GDN + 1], None,
                                      ALU.mult).then_inc(s_gt.freed(k)[0], 1)
                for i in range(2 * NJ):
                    j, f = i // 2, i % 2
                    dve.wait_ge(*s_go.full(i + 1))
                    hv = h[:, j, f * HALF:(f + 1) * HALF]
                    dve.tensor_tensor(hv, hv, psum[:, banks.bank(s_go, i), :], ALU.add).then_inc(s_go.freed(i)[0], 1)
                s_go.wait_read(dve, 2 * NJ - 1)
                dve.sem_inc(h_done, 1)

            for l in LAYERS:
                if l == 1:
                    gdn_dve()
                L = lay[l]
                norm(f"ffn{l}")
                xt_out(dve, "dve", L.s_xt, ROW_FFN + 8 * l)
                for j in range(NJ):
                    dve.wait_ge(*L.s_lg.full(j + 1))
                    lg = psum[:, banks.bank(L.s_lg, j), 0:NE]
                    link(dve.tensor_reduce(rs[:, 12:13], lg, AX_X, ALU.max))
                    dve.tensor_scalar(work[:, 512 + 16 * j:528 + 16 * j], lg, rs[:, 12:13], None, ALU.subtract).then_inc(soft_n, 1)
                    dve.wait_ge(soft_e, 4 * l + j + 1)
                    dve.sem_inc(L.s_lg.freed(j)[0], 1)
                    link(dve.reciprocal(rs[:, 13:14], ss[:, 20 + j:21 + j]))
                    a = aff[:, j % NT, j // NT, :]
                    dve.tensor_scalar(a, a, rs[:, 13:14], None, ALU.mult).then_inc(soft_n, 1)
                dve.wait_ge(*L.s_at.full(1))
                dve.tensor_copy(afft, psum[0:32, banks.bank(L.s_at, 0), 0:SEQ]).then_inc(L.s_at.freed(0)[0], 1)
                L.s_at.wait_read(dve, 0)
                for r in range(CAP // 8):
                    v8, i8 = topv[:, 8 * r:8 * r + 8], topi[:, 8 * r:8 * r + 8]
                    link(dve.max(v8, afft))
                    link(dve.max_index(i8, v8, afft))
                    if r < CAP // 8 - 1:
                        link(dve.match_replace(afft, v8, afft, -1.0))
                dve.tensor_copy(topf[:, :], topi[:, :]).then_inc(top_done, 1)
                dve.wait_ge(top_done, l + 1)
                dve.tensor_tensor(spread, topf[:, :].unsqueeze(1).to_broadcast([32, 32, CAP]),
                                  diag32[:, :].unsqueeze(2).to_broadcast([32, 32, CAP]), ALU.mult).then_inc(spread_done, 1)
                dve.wait_ge(*L.s_gt.full(1))
                g0 = psum[0:32, banks.bank(L.s_gt, 0), :]
                for i in range(GRP):
                    ins = dve.tensor_copy(gcol[32 * i:32 * i + 32, :, :],
                                          g0[:, 0:NS * NE].rearrange("p (s q e) -> p q s e", s=NS, q=NQ)[:, :, :, i])
                link(ins)
                dve.sem_inc(L.s_gt.freed(0)[0], 1)
                dve.sem_inc(gcol_done, 1)
                for s in range(NS):
                    dve.wait_ge(*L.s_ib.full(s + 1))
                    for t in range(NT):
                        dve.tensor_scalar(oh[:, NT * s + t, :], psum[:, banks.bank(L.s_ib, s), :],
                                          token[:, t:t + 1], None, ALU.is_equal).then_inc(onehot_done, 1)
                    dve.wait_ge(onehot_done, 4 * l + 2 * s + 2)
                    dve.sem_inc(L.s_ib.freed(s)[0], 1)
                for q in range(1, NQ, 2):
                    dve.wait_ge(*L.s_st.full(q + 1))
                    for s in range(NS):
                        ins = dve.tensor_scalar(sc[:, q, 2 * s:2 * s + 2, :], psum[:, banks.bank(L.s_st, q), s * SEQ:(s + 1) * SEQ],
                                                gcol[:, q, s:s + 1], None, ALU.mult)
                    ins.then_inc(L.s_st.freed(q)[0], 1)
                if l == 0:
                    dve.sem_inc(moe_sem["scat_free"], 4)
                    dve.sem_inc(moe_sem["w_used"], NSPL)
                def gather_lo(q):
                    for kk in range(KD):
                        src = psum[:, kk // 2, (kk % 2) * 256:(kk % 2 + 1) * 256].rearrange("p (s e c) -> p e s c", s=NS, e=GRP)
                        if kk % 2 == 0:
                            dve.wait_ge(moe_sem["gather_hi"], q * 16 + 2 * kk + 4 + L.done["gather_hi"])
                        for s in range(NS):
                            dve.scalar_tensor_tensor(out=xsplit[:, kk, :, 1, s * CAP:(s + 1) * CAP], in0=src[:, :, s, :],
                                                     scalar=gains[:, ROW_FFN + 8 * l + kk:ROW_FFN + 8 * l + kk + 1],
                                                     in1=xsplit[:, kk, :, 0, s * CAP:(s + 1) * CAP].bitcast(F32),
                                                     op0=ALU.mult, op1=ALU.subtract).then_inc(moe_sem["gather_lo"], 1)

                def step(q, last_step):
                    def pre_out(i, u):
                        kind, f = ("gate", "up")[u % 2], u // 2
                        dve.wait_ge(moe_sem["w_used"], unit_done(L, q, unit_of[(kind, i, f)]))
                        if i and u == 0:
                            dve.wait_ge(moe_sem["folded"], q * (2 * GRP) + 2 * i + L.done["folded"])
                        dve.tensor_copy(pre[:, u, :], psum[:, u, :]).then_inc(moe_sem["pre_read"], 1)

                    def hidden(i):
                        dve.wait_ge(moe_sem["silu_done"], q * GRP + (i + 1) + L.done["silu_done"])
                        dve.wait_ge(moe_sem["folded"], q * (2 * GRP) + 2 * i + 2 + L.done["folded"])
                        dve.tensor_tensor(hid, sg, turned[1], ALU.mult).then_inc(moe_sem["hid_done"], 1)

                    def hidden_lo(i):
                        dve.wait_ge(moe_sem["hid_hi"], q * GRP + (i + 1) + L.done["hid_hi"])
                        dve.tensor_tensor(hsplit[:, i % 2, :, 1, :], hid, hsplit[:, i % 2, :, 0, :].bitcast(F32),
                                          ALU.subtract).then_inc(moe_sem["hid_lo"], 1)

                    def y_lo(i, f):
                        dve.wait_ge(moe_sem["y_hi"], q * 16 + 4 * i + 2 * f + 2 + L.done["y_hi"])
                        for s in range(NS):
                            y = ybuf[32 * i:32 * i + 32, s, f * HALF:(f + 1) * HALF]
                            dve.tensor_tensor(y, psum[64 + 32 * s:96 + 32 * s, 4 + f, :], y, ALU.add).then_inc(moe_sem["y_lo"], 1)

                    for m in range(NSPL, NH + NSPL):
                        if owner[m % NH] == "dve" and (m < NH or not last_step):
                            split_lo(dve, L, q + m // NH, m % NH)
                        for i in range(GRP):
                            for u, (kind, f) in enumerate((("gate", 0), ("up", 0), ("gate", 1), ("up", 1))):
                                if m == 2 * unit_of[(kind, i, f)] + 4:
                                    pre_out(i, u)
                            last = 2 * unit_of[("up", i, 1)] - (i == GRP - 1)
                            if m == last + 7:
                                hidden(i)
                            if m == last + 8:
                                hidden_lo(i)
                            for f in range(2):
                                if m == min(NH + NSPL - 1, 2 * unit_of[("down", i, f)] + 5):
                                    y_lo(i, f)
                    if not last_step:
                        gather_lo(q + 1)
                    for g in range(8):
                        j, f = g // 2, g % 2
                        dve.wait_ge(moe_sem["scat_in_psum"], q * 8 + (g + 1) + L.done["scat_in_psum"])
                        hv = h[:, j, f * HALF:(f + 1) * HALF]
                        dve.tensor_tensor(hv, hv, psum[:, 4 + g % 4, :], ALU.add).then_inc(moe_sem["scat_free"], 1)

                for m in range(NSPL):
                    if owner[m] == "dve":
                        split_lo(dve, L, 0, m)
                gather_lo(0)
                with dve.Fori(0, NQ - 1) as q:
                    step(q, False)
                step(NQ - 1, True)
                dve.wait_ge(moe_sem["scat_free"], 8 * NQ + 4 + L.done["scat_free"])
                dve.sem_inc(h_done, 1)
                norm(f"ple{l}")
                xt_out(dve, "dve", L.s_pxt, ROW_PLE + 8 * l)
                for k in range(2):
                    copy_out(L.s_ppt, k, ptt[:, k, :])
                for i in range(8):
                    j, f = i // 2, i % 2
                    dve.wait_ge(*L.s_pg.freed(i))
                    dve.wait_ge(*L.s_pp.full(i + 1))
                    dve.tensor_tensor(prod[:, i % 2, :], gate[:, i % 2, :], psum[:, banks.bank(L.s_pp, i), :],
                                      ALU.mult).then_inc(L.s_pp.freed(i)[0], 1)
                    dve.wait_ge(*L.s_pp.freed(i))
                    hv = h[:, j, f * HALF:(f + 1) * HALF]
                    link(dve.tensor_tensor(hv, hv, prod[:, i % 2, :], ALU.add))
                dve.sem_inc(h_done, 1)
            norm("last")
            dve.wait_ge(fg_in, 16)
            dve.wait_ge(xn_done, NJ * len(norms))
            for j in range(NJ):
                dve.tensor_tensor(xn[:, j, :], xn[:, j, :], fg, ALU.mult).then_inc(out_ready, 1)


_ORDER = ['x_prompt', 'x_sample', 'p_prompt', 'p_sample', 'norm_mix_g', 'norm_ffn_g', 'norm_ple_g',
          'final_norm_g', 'mla_w_in', 'mla_q_norm_g', 'mla_w_qb', 'mla_kv_norm_g', 'mla_w_kvb', 'mla_w_out',
          'gdn_w_in', 'gdn_conv_w', 'gdn_A_log', 'gdn_dt_bias', 'gdn_norm_g', 'gdn_w_out',
          'moe_w_router', 'moe_w_gate', 'moe_w_up', 'moe_w_down', 'ple_w_proj', 'ple_w_gate']


def kernel(**inputs):
    import concourse.bacc as _bacc
    from concourse.bass_utils import run_bass_kernel_spmd as _run

    inv = 10000.0 ** (-np.arange(0, ROPE, 2, dtype=np.float32) / ROPE)
    ang = np.arange(SEQ, dtype=np.float32)[:, None] * inv[None, :].astype(np.float32)
    tables = {"rope_cos": np.cos(ang).astype(np.float32), "rope_sin": np.sin(ang).astype(np.float32)}
    nc = _bacc.Bacc("TRN2", target_bir_lowering=False, num_devices=1, dynamic_dma_scratch_size=4096)
    arrays, args = {}, []
    for name in _ORDER + list(tables):
        a = tables[name] if name in tables else np.ascontiguousarray(inputs[name])
        arrays[f"in_{name}"] = a
        args.append(nc.dram_tensor(f"in_{name}", a.shape, mybir.dt.from_np(a.dtype), kind="ExternalInput").ap())
    for name in ("y_prompt", "y_sample"):
        args.append(nc.dram_tensor(f"out_{name}", (1, SEQ, D), F32, kind="ExternalOutput").ap())
    trunk_kernel(nc, *args)
    r = _run(nc, [arrays], core_ids=[0])
    return r.results[0]["out_y_prompt"], r.results[0]["out_y_sample"]
```
